# Optimizing a Trainium2 kernel written in Bass

```python
import jax, jax.numpy as jnp
from jax import lax
import numpy as np

D_MODEL = 1024
BATCH = 1
SEQ = 2048
DEPTH = 1

CHUNK = 64
D_MIX = D_MODEL
HEAD_DIM = 64
D_ATTN = D_MIX // 2
N_Q_HEADS = D_ATTN // HEAD_DIM
N_KV_HEADS = 2
Q_PER_KV = N_Q_HEADS // N_KV_HEADS
WINDOW = 128
WINDOW_CHUNKS = WINDOW // CHUNK
ROPE_THETA = 500000.0
ROPE_DIM = HEAD_DIM // 4
D_CONV = D_MIX - D_ATTN
CONV_WIDTH = 31
D_FF = 2816
FFN_CONV_WIDTH = 3
LN_EPS = 1e-5
ALPHA = (2.0 * DEPTH) ** 0.25
BETA = (8.0 * DEPTH) ** -0.25
Q_END = N_Q_HEADS * HEAD_DIM
K_END = Q_END + N_KV_HEADS * HEAD_DIM
V_END = K_END + N_KV_HEADS * HEAD_DIM
D_IN = V_END + 2 * D_CONV
MAX_POS_OFFSET = 100000

kernel_name = "hymba_conformer_swa_sink_convffn_deepnorm"

def layer_norm(x, g, b):
    xf = x.astype(jnp.float32)
    mu = jnp.mean(xf, axis=-1, keepdims=True)
    var = jnp.mean(jnp.square(xf - mu), axis=-1, keepdims=True)
    y = (xf - mu) * lax.rsqrt(var + LN_EPS)
    return (y * g.astype(jnp.float32) + b.astype(jnp.float32)).astype(x.dtype)

def causal_depthwise_conv(x, w, b):
    k = w.shape[0]
    y = lax.conv_general_dilated(
        x, w[:, None, :].astype(x.dtype), window_strides=(1,), padding=[(k - 1, 0)],
        dimension_numbers=('NWC', 'WIO', 'NWC'), feature_group_count=x.shape[-1])
    return y + b.astype(x.dtype)

def partial_rotary(x, positions):
    half = ROPE_DIM // 2
    inv_freq = jnp.float32(ROPE_THETA) ** (-jnp.arange(half, dtype=jnp.float32) / half)
    ang = positions.astype(jnp.float32)[..., None] * inv_freq
    cos = jnp.cos(ang)[:, :, None, :]
    sin = jnp.sin(ang)[:, :, None, :]
    xr = x[..., :ROPE_DIM].astype(jnp.float32)
    x1, x2 = xr[..., :half], xr[..., half:]
    rot = jnp.concatenate([x1 * cos - x2 * sin, x2 * cos + x1 * sin], axis=-1).astype(x.dtype)
    return jnp.concatenate([rot, x[..., ROPE_DIM:]], axis=-1)

def swa_gqa_with_sinks(q, k, v, sinks):
    B, S = q.shape[0], q.shape[1]
    nc = S // CHUNK
    qc = q.reshape(B, nc, CHUNK, N_KV_HEADS, Q_PER_KV, HEAD_DIM)

    def band(t):
        tc = t.reshape(B, nc, CHUNK, N_KV_HEADS, HEAD_DIM)
        tp = jnp.pad(tc, ((0, 0), (WINDOW_CHUNKS - 1, 0), (0, 0), (0, 0), (0, 0)))
        return jnp.concatenate([tp[:, j:j + nc] for j in range(WINDOW_CHUNKS)], axis=2)

    kb, vb = band(k), band(v)
    scores = jnp.einsum('bcqhgd,bckhd->bchgqk', qc, kb,
                        preferred_element_type=jnp.float32) * (HEAD_DIM ** -0.5)
    key_chunk = (jnp.arange(nc)[:, None] - (WINDOW_CHUNKS - 1)
                 + jnp.arange(WINDOW)[None, :] // CHUNK)
    valid = (key_chunk >= 0)[None, :, None, None, None, :]
    scores = jnp.where(valid, scores, jnp.finfo(jnp.float32).min)
    sink = jnp.broadcast_to(
        sinks.astype(jnp.float32).reshape(N_KV_HEADS, Q_PER_KV)[None, None, :, :, None, None],
        scores.shape[:-1] + (1,))
    probs = jax.nn.softmax(jnp.concatenate([scores, sink], axis=-1), axis=-1)[..., :WINDOW]
    out = jnp.einsum('bchgqk,bckhd->bcqhgd', probs.astype(v.dtype), vb)
    return out.reshape(B, S, N_Q_HEADS * HEAD_DIM)

def conformer_conv(u, conv_w, conv_b, ln_g, ln_b):
    a, gate = jnp.split(u, 2, axis=-1)
    h = a * jax.nn.sigmoid(gate)
    h = causal_depthwise_conv(h, conv_w, conv_b)
    h = layer_norm(h, ln_g, ln_b)
    return jax.nn.silu(h)

def conv_gated_mlp(h, w_up, conv_w, conv_b, w_down):
    z = causal_depthwise_conv(h @ w_up, conv_w, conv_b)
    g, val = jnp.split(z, 2, axis=-1)
    return (jax.nn.gelu(g, approximate=False) * val) @ w_down

def setup_inputs(seed: int = 0) -> dict:
    key = jax.random.key(seed)
    ks = jax.random.split(key, 20)
    f32 = jnp.float32
    L = DEPTH

    def nrm(k, shape, scale):
        return jax.random.normal(k, shape, f32) * scale

    x = jax.random.normal(ks[0], (BATCH, SEQ, D_MODEL), f32)
    offsets = jax.random.randint(ks[1], (BATCH, 1), 0, MAX_POS_OFFSET, dtype=jnp.int32)
    positions = offsets + jnp.arange(SEQ, dtype=jnp.int32)[None, :]
    in_ln_g = 1.0 + nrm(ks[2], (D_MODEL,), 0.02)
    in_ln_b = nrm(ks[3], (D_MODEL,), 0.02)
    col_scale = jnp.concatenate([jnp.ones((K_END,), f32),
                                 jnp.full((V_END - K_END,), BETA, f32),
                                 jnp.ones((D_IN - V_END,), f32)])
    w_in = nrm(ks[4], (L, D_MODEL, D_IN), D_MODEL ** -0.5) * col_scale
    sinks = nrm(ks[5], (L, N_Q_HEADS), 0.5)
    conv_w = nrm(ks[6], (L, CONV_WIDTH, D_CONV), CONV_WIDTH ** -0.5)
    conv_b = nrm(ks[7], (L, D_CONV), 0.02)
    conv_ln_g = 1.0 + nrm(ks[8], (L, D_CONV), 0.02)
    conv_ln_b = nrm(ks[9], (L, D_CONV), 0.02)
    w_o = nrm(ks[10], (L, D_MIX, D_MODEL), BETA * D_MIX ** -0.5)
    ln1_g = 1.0 + nrm(ks[11], (L, D_MODEL), 0.02)
    ln1_b = nrm(ks[12], (L, D_MODEL), 0.02)
    w_up = nrm(ks[13], (L, D_MODEL, 2 * D_FF), D_MODEL ** -0.5)
    ffn_conv_w = nrm(ks[14], (L, FFN_CONV_WIDTH, 2 * D_FF), FFN_CONV_WIDTH ** -0.5)
    ffn_conv_b = nrm(ks[15], (L, 2 * D_FF), 0.02)
    w_down = nrm(ks[16], (L, D_FF, D_MODEL), BETA * D_FF ** -0.5)
    ln2_g = 1.0 + nrm(ks[17], (L, D_MODEL), 0.02)
    ln2_b = nrm(ks[18], (L, D_MODEL), 0.02)
    return {"x": x, "positions": positions, "in_ln_g": in_ln_g, "in_ln_b": in_ln_b,
            "w_in": w_in, "sinks": sinks, "conv_w": conv_w, "conv_b": conv_b,
            "conv_ln_g": conv_ln_g, "conv_ln_b": conv_ln_b, "w_o": w_o,
            "ln1_g": ln1_g, "ln1_b": ln1_b, "w_up": w_up, "ffn_conv_w": ffn_conv_w,
            "ffn_conv_b": ffn_conv_b, "w_down": w_down, "ln2_g": ln2_g, "ln2_b": ln2_b}

def reference(x, positions, in_ln_g, in_ln_b, w_in, sinks, conv_w, conv_b,
              conv_ln_g, conv_ln_b, w_o, ln1_g, ln1_b, w_up, ffn_conv_w,
              ffn_conv_b, w_down, ln2_g, ln2_b):
    B, S, _ = x.shape
    h = layer_norm(x, in_ln_g, in_ln_b)
    for l in range(DEPTH):
        proj = h @ w_in[l]
        q, k, v, u = jnp.split(proj, [Q_END, K_END, V_END], axis=-1)
        q = partial_rotary(q.reshape(B, S, N_Q_HEADS, HEAD_DIM), positions)
        k = partial_rotary(k.reshape(B, S, N_KV_HEADS, HEAD_DIM), positions)
        v = v.reshape(B, S, N_KV_HEADS, HEAD_DIM)
        attn = swa_gqa_with_sinks(q, k, v, sinks[l])
        conv = conformer_conv(u, conv_w[l], conv_b[l], conv_ln_g[l], conv_ln_b[l])
        mix = jnp.concatenate([attn, conv], axis=-1) @ w_o[l]
        h = layer_norm(ALPHA * h + mix, ln1_g[l], ln1_b[l])
        ffn = conv_gated_mlp(h, w_up[l], ffn_conv_w[l], ffn_conv_b[l], w_down[l])
        h = layer_norm(ALPHA * h + ffn, ln2_g[l], ln2_b[l])
    return h


_drawn_inputs = setup_inputs


def setup_inputs(seed=0):
    import zlib

    import numpy as np

    out = dict(_drawn_inputs(seed))
    spreads = {}
    factors = {'in_ln_b': 2.818,
     'sinks': 64.0,
     'conv_b': 6.649,
     'conv_ln_g': 8.0,
     'conv_ln_b': 21.428,
     'ln1_g': 2.698,
     'ln1_b': 2.759,
     'ffn_conv_b': 6.421,
     'ln2_g': 8.2,
     'ln2_b': 8.342}
    for name, (base, spread) in spreads.items():
        noise = np.random.default_rng([zlib.crc32(name.encode()), seed]).standard_normal(out[name].shape)
        drawn = base * np.exp(spread * noise) if base else spread * noise
        out[name] = __import__('jax').numpy.asarray(drawn.astype(out[name].dtype))
    for name, factor in factors.items():
        out[name] = (out[name] * factor).astype(out[name].dtype)
    return out
```

```python
from contextlib import ExitStack

import numpy as np
import concourse.bass as bass
from concourse import mybir

F32 = mybir.dt.float32
F32R = mybir.dt.float32r
I32 = mybir.dt.int32
ALU = mybir.AluOpType
ACT = mybir.ActivationFunctionType
AX = mybir.AxisListType

P = 128
SEQ = 2048
D = 1024
HEAD = 64
CHUNK = 64
NQ, NKV = 8, 2
QKV = (NQ + 2 * NKV) * HEAD
DC = 512
TAPS = 31
HALO = TAPS - 1
DFF = 2816
FTAPS = 3
EPS = 1e-5
ROT = HEAD // 4
ROPE_THETA = 500000.0
ALPHA = 2.0 ** 0.25
KT = D // P
NT = SEQ // P
BLK = 512
NB = SEQ // BLK
RB = BLK // P
CT = DC // P
QT = QKV // P
FT = DFF // P
HALF = FT // 2

IN_TILES = []
for _j in range(CT):
    IN_TILES += [QT + _j, QT + CT + _j]
    if _j:
        IN_TILES += [2 * _j - 2, 2 * _j - 1]

PAR_TAPS = 0
PAR_CB = PAR_TAPS + CT * TAPS
PAR_LNG = PAR_CB + CT
PAR_LNB = PAR_LNG + CT
PAR_FTAPS = PAR_LNB + CT
PAR_FB = PAR_FTAPS + 2 * FT * FTAPS
PAR_SINK = PAR_FB + 2 * FT
PAR_N = PAR_SINK + NKV * 4
CON_ID, CON_ROT, CON_ONES, CON_FREQ = 0, P, 2 * P, 3 * P
CON_N = 3 * P + 4


class Count:

    def __init__(self, sem, eng):
        self.sem, self.eng, self.base, self.n = sem, eng, 0, 0

    def inc(self, ins):
        ins.then_inc(self.sem, 1)
        self.n += 1
        return self.n

    def wait(self, n=None):
        self.eng.wait_ge(self.sem, self.base + (self.n if n is None else n))


def row_to_all(ap):
    return ap.rearrange("(o n) -> o n", o=1).broadcast_to([P, ap.shape[0]])


def refine_rstd(nc, chain, rstd, v, y, t):
    chain.wait()
    chain.inc(nc.vector.tensor_tensor(t, y, y, ALU.mult))
    chain.wait()
    chain.inc(nc.vector.scalar_tensor_tensor(out=t, in0=t, scalar=-0.5, in1=v, op0=ALU.mult, op1=ALU.mult))
    chain.wait()
    chain.inc(nc.vector.scalar_tensor_tensor(out=rstd, in0=t, scalar=1.5, in1=y, op0=ALU.add, op1=ALU.mult))


def phase_project(nc, x, ln_g, ln_b, w_tiles, par, con, h_scr, qkv_scr, conv_scr):
    ctx = ExitStack()
    with ctx:
        def sb(name, shape, dt=F32):
            return ctx.enter_context(nc.sbuf_tensor(name, shape, dt))

        def sem(name):
            return ctx.enter_context(nc.semaphore(name))

        hT_hi = sb("a_hT_hi", [P, KT, SEQ], F32R)
        hT_lo = sb("a_hT_lo", [P, KT, SEQ], F32R)
        w_raw = sb("a_w_raw", [P, 2, KT, P])
        w_hi = sb("a_w_hi", [P, 2, KT, P], F32R)
        w_lo = sb("a_w_lo", [P, 2, KT, P], F32R)
        glu = sb("a_glu", [P, 2, HALO + SEQ])
        sig = sb("a_sig", [P, BLK])
        q_out = sb("a_q_out", [P, 2, BLK])
        xs = sb("a_xs", [P, RB, D])
        conv_out = xs[:, :, :].rearrange("p (s a) d -> p s (a d)", s=2)
        g_bc = sb("a_g", [P, D])
        b_bc = sb("a_b", [P, D])
        ident = sb("a_ident", [P, P])
        taps = sb("a_taps", [P, CT, TAPS])
        cbias = sb("a_cbias", [P, CT])
        stat = sb("a_stat", [P, RB, 2, 6])
        mv = sb("a_mv", [P, RB, 2])
        vs = sb("a_vs", [P, 5, RB])
        veps, root, inv, tmp, rstd = (vs[:, k, :] for k in range(5))
        nmr = sb("a_nmr", [P, RB])
        mm = [ctx.enter_context(nc.psum_tensor(f"a_mm{k}", [P, BLK], F32)) for k in range(4)]
        acc = ctx.enter_context(nc.psum_tensor("a_acc", [P, SEQ], F32))
        tp = [acc[:, k * D:(k + 1) * D].rearrange("p (k t) -> p k t", k=KT) for k in range(2)]

        con_ld, par_ld = sem("a_con_ld"), sem("a_par_ld")
        x_ld = [sem(f"a_x_ld{r}") for r in range(RB)]
        h_st = [sem(f"a_h_st{r}") for r in range(RB)]
        w_ld = [sem(f"a_w_ld{s}") for s in range(2)]
        veps_ok, root_ok, nmr_ok = sem("a_veps"), sem("a_root"), sem("a_nmr")
        norm_ok, scaled_ok, h_ok = sem("a_norm"), sem("a_scaled"), sem("a_h")
        tp_ok, tp_free, hi_ok, lo_ok = sem("a_tp"), sem("a_tp_free"), sem("a_hi"), sem("a_lo")
        whi_ok, wlo_ok = sem("a_whi"), sem("a_wlo")
        mm_ok, mm_free = sem("a_mm"), sem("a_mm_free")
        pad_ok, glu_ok = sem("a_pad"), sem("a_glu")
        conv_ok, conv_free, dve_seq = sem("a_conv"), sem("a_conv_free"), sem("a_dve")
        stats_seen = sem("a_stats_seen")
        q_st = [sem(f"a_q_st{s}") for s in range(2)]
        c_st = [sem(f"a_c_st{s}") for s in range(2)]
        block = ctx.enter_context(nc.Block())

        @block.sync
        def _(sp):
            sp.dma_start(ident[:], con[:, CON_ID:CON_ID + P]).then_inc(con_ld, 16)
            for r in range(RB):
                sp.dma_start(xs[:, r, :], x[bass.ts(r, P), :]).then_inc(x_ld[r], 16)
            sp.dma_start(g_bc[:], row_to_all(ln_g)).then_inc(par_ld, 16)
            sp.dma_start(b_bc[:], row_to_all(ln_b)).then_inc(par_ld, 16)
            sp.dma_start(taps[:], par[:, PAR_TAPS:PAR_TAPS + CT * TAPS].rearrange("p (c t) -> p c t", c=CT)).then_inc(par_ld, 16)
            sp.dma_start(cbias[:], par[:, PAR_CB:PAR_CB + CT]).then_inc(par_ld, 16)
            for s in range(2):
                sp.dma_start(w_raw[:, s, :, :], w_tiles[s, :, :, :]).then_inc(w_ld[s], 16)

            def reload(n, r):
                sp.wait_ge(h_st[r], n * 16 + 16)
                sp.wait_ge(tp_ok, RB * n + (r + 1))
                sp.dma_start(xs[:, r, :], x[bass.ds((n * RB + (RB + r)) * P, P), :]).then_inc(x_ld[r], 16)

            def store(n, r):
                sp.wait_ge(h_ok, RB * n + (r + 1))
                sp.dma_start(h_scr[bass.ds(RB * n + r, 1), :, :].rearrange("o p d -> p (o d)"), xs[:, r, :]).then_inc(h_st[r], 16)

            with sp.Fori(0, NB - 1) as n:
                for r in range(RB):
                    store(n, r)
                    if r:
                        reload(n, r - 1)
                reload(n, RB - 1)
            for r in range(RB):
                store(NB - 1, r)
            with sp.Fori(0, CT - 1) as j:
                for u in range(4):
                    sp.wait_ge(wlo_ok, 4 * j + (u + 1))
                    sp.dma_start(w_raw[:, u % 2, :, :], w_tiles[bass.ds(4 * j + (u + 2), 1), :, :, :].rearrange("o p k c -> p (o k) c")).then_inc(w_ld[u % 2], 16)
            for r in range(RB):
                sp.wait_ge(h_st[r], 16 * NB)

        @block.scalar
        def _(act):
            def weights_hi(nth, slot):
                act.wait_ge(w_ld[slot], nth * 16)
                nc.scalar.copy(w_hi[:, slot, :, :], w_raw[:, slot, :, :]).then_inc(whi_ok, 1)

            def norm(n):
                act.wait_ge(veps_ok, n + 1)
                nc.scalar.activation(root, veps, ACT.Sqrt).then_inc(root_ok, 1)
                act.wait_ge(nmr_ok, n + 1)
                for r in range(RB):
                    nc.scalar.activation(xs[:, r, :], xs[:, r, :], ACT.Identity, bias=nmr[:, r:r + 1],
                                         scale=rstd[:, r:r + 1]).then_inc(norm_ok, 1)

            def hi_of(n, r):
                act.wait_ge(tp_ok, RB * n + (r + 1))
                nc.scalar.copy(hT_hi[:, :, bass.ds((RB * n + r) * P, P)], tp[r % 2]).then_inc(hi_ok, 1)

            def take_a(e, slot, col, bank):
                act.wait_ge(mm_ok, e + 1)
                nc.scalar.copy(glu[:, slot, bass.ds(col, BLK)], mm[bank][:]).then_inc(mm_free, 1)

            def take_gate(e, k, bank):
                act.wait_ge(mm_ok, e + 1)
                act.wait_ge(glu_ok, k + 1)
                nc.scalar.activation(sig[:], mm[bank][:], ACT.Sigmoid).then_inc(mm_free, 1)

            act.sem_inc(mm_free, 2)
            act.sem_inc(conv_ok, 1)
            act.sem_inc(q_st[0], 16)
            act.sem_inc(q_st[1], 16)
            weights_hi(1, 0)
            weights_hi(1, 1)
            norm(0)
            for r in range(RB):
                hi_of(0, r)
            with act.Fori(1, NB) as n:
                norm(n)
                hi_of(n, 0)
                hi_of(n, 1)
                take_a(2 * n - 2, 0, n * BLK + (HALO - BLK), 2)
                hi_of(n, 2)
                hi_of(n, 3)
                take_gate(2 * n - 1, n - 1, 3)
            take_a(2 * NB - 2, 0, (NB - 1) * BLK + HALO, 2)
            take_gate(2 * NB - 1, NB - 1, 3)
            act.wait_ge(mm_ok, 2 * NB)
            weights_hi(2, 0)
            weights_hi(2, 1)
            for r in range(RB):
                act.wait_ge(h_st[r], 16 * NB)
            act.sem_inc(conv_free, 32)

            def projections(j, last):
                e0 = 4 * NB * j + 2 * NB
                act.wait_ge(conv_ok, j + 1)
                for n in range(NB):
                    take_a(e0 + n, (j + 1) % 2, n * BLK + HALO, n)
                weights_hi(2 * j + 3, 0)
                for n in range(NB):
                    take_gate(e0 + (NB + n), NB * j + (NB + n), n)
                weights_hi(2 * j + 3, 1)

                def store_q(k):
                    act.wait_ge(mm_free, e0 + (2 * NB + k + 3))
                    dst = qkv_scr[bass.ds(2 * j + k // NB, 1), :, bass.ts(k % NB, BLK)]
                    act.dma_start(dst.rearrange("o p t -> p (o t)"), q_out[:, k % 2, :]).then_inc(q_st[k % 2], 16)

                for k in range(2 * NB):
                    act.wait_ge(mm_ok, e0 + (2 * NB + k + 1))
                    act.wait_ge(q_st[k % 2], 16 * NB * j + 16 * (k // 2 + 1))
                    nc.scalar.copy(q_out[:, k % 2, :], mm[k % NB][:]).then_inc(mm_free, 1)
                    if k:
                        store_q(k - 1)
                    if k % NB == NB - 1 and not last:
                        weights_hi(2 * j + 4, k // NB)
                store_q(2 * NB - 1)
                store_conv(j)

            def store_conv(j):
                act.wait_ge(conv_ok, j + 2)
                act.dma_start(conv_scr[bass.ds(j, 1), :, :].rearrange("o p t -> p (o t)"),
                              conv_out[:, j % 2, :]).then_inc(conv_free, 16)

            with act.Fori(0, CT - 2) as j:
                projections(j, False)
            projections(CT - 2, True)
            store_conv(CT - 1)
            act.wait_ge(conv_free, 16 * (CT + 2))
            for s in range(2):
                act.wait_ge(q_st[s], 16 * (NB * (CT - 1) + 1))

        @block.gpsimd
        def _(pool):
            nc.gpsimd.memset(glu[:, :, 0:HALO], 0.0).then_inc(glu_ok, 1)

            def weights_lo(s, slot):
                pool.wait_ge(whi_ok, s + 1)
                nc.gpsimd.tensor_tensor(w_lo[:, slot, :, :], w_raw[:, slot, :, :], w_hi[:, slot, :, :].bitcast(F32),
                                        ALU.subtract).then_inc(wlo_ok, 1)

            def add_bias(n):
                for r in range(RB):
                    pool.wait_ge(scaled_ok, RB * n + (r + 1))
                    nc.gpsimd.tensor_tensor(xs[:, r, :], xs[:, r, :], b_bc[:], ALU.add).then_inc(h_ok, 1)

            def gate(e, slot, col):
                pool.wait_ge(mm_free, e + 3)
                v = glu[:, slot, bass.ds(col, BLK)]
                nc.gpsimd.tensor_tensor(v, v, sig[:], ALU.mult).then_inc(glu_ok, 1)

            weights_lo(0, 0)
            weights_lo(1, 1)
            pool.wait_ge(par_ld, 64)
            add_bias(0)
            with pool.Fori(1, NB) as n:
                add_bias(n)
                gate(2 * n - 1, 0, n * BLK + (HALO - BLK))
            gate(2 * NB - 1, 0, (NB - 1) * BLK + HALO)
            weights_lo(2, 0)
            weights_lo(3, 1)

            def projections(j, last):
                weights_lo(4 * j + 4, 0)
                for n in range(NB):
                    gate(4 * NB * j + (3 * NB + n), (j + 1) % 2, n * BLK + HALO)
                weights_lo(4 * j + 5, 1)
                if not last:
                    weights_lo(4 * j + 6, 0)
                    weights_lo(4 * j + 7, 1)

            with pool.Fori(0, CT - 2) as j:
                projections(j, False)
            projections(CT - 2, True)

        @block.vector
        def _(dve):
            chain = Count(dve_seq, dve)
            dve.wait_ge(par_ld, 64)

            STEPS = 2 * RB + RB + 4
            with dve.Fori(0, NB) as n:
                chain.base, chain.n = n * STEPS, 0
                for r in range(RB):
                    dve.wait_ge(x_ld[r], n * 16 + 16)
                    for a in range(2):
                        chain.inc(nc.vector.bn_stats(stat[:, r, a, :], xs[:, r, a * BLK:(a + 1) * BLK]))
                chain.wait()
                dve.sem_inc(stats_seen, 1)
                for r in range(RB):
                    chain.inc(nc.vector.bn_aggr(mv[:, r, :], stat[:, r, :, :].rearrange("p a s -> p (a s)")))
                chain.wait()
                nc.vector.tensor_scalar(veps, mv[:, :, 1], EPS, None, ALU.add).then_inc(veps_ok, 1)
                dve.wait_ge(root_ok, n + 1)
                chain.inc(nc.vector.reciprocal(inv, root))
                dve.wait_ge(veps_ok, n + 1)
                refine_rstd(nc, chain, rstd, veps, inv, tmp)
                chain.wait()
                nc.vector.scalar_tensor_tensor(out=nmr[:], in0=mv[:, :, 0], scalar=-1.0, in1=rstd, op0=ALU.mult,
                                               op1=ALU.mult).then_inc(nmr_ok, 1)
                assert chain.n == STEPS
                for r in range(RB):
                    dve.wait_ge(norm_ok, RB * n + (r + 1))
                    nc.vector.tensor_tensor(xs[:, r, :], xs[:, r, :], g_bc[:], ALU.mult).then_inc(scaled_ok, 1)
                for r in range(RB):
                    dve.wait_ge(hi_ok, RB * n + (r + 1))
                    nc.vector.tensor_tensor(hT_lo[:, :, bass.ds((RB * n + r) * P, P)], tp[r % 2],
                                            hT_hi[:, :, bass.ds((RB * n + r) * P, P)].bitcast(F32),
                                            ALU.subtract).then_inc(lo_ok, 1)

            with dve.Fori(0, CT) as j:
                dve.wait_ge(glu_ok, NB * j + (NB + 1))
                chain.base, chain.n = j * (TAPS - 1) + NB * STEPS, 0
                dve.wait_ge(conv_ok, j + 1)
                chain.inc(nc.vector.tensor_scalar(acc[:], glu[:, bass.ds(j % 2, 1), 0:SEQ].rearrange("p o t -> p (o t)"),
                                                  taps[:, bass.ds(j, 1), 0:1].rearrange("p o t -> p (o t)"),
                                                  cbias[:, bass.ds(j, 1)], ALU.mult, ALU.add))
                for k in range(1, TAPS):
                    chain.wait()
                    src = glu[:, bass.ds(j % 2, 1), k:k + SEQ].rearrange("p o t -> p (o t)")
                    tap = taps[:, bass.ds(j, 1), k:k + 1].rearrange("p o t -> p (o t)")
                    if k < TAPS - 1:
                        chain.inc(nc.vector.scalar_tensor_tensor(out=acc[:], in0=src, scalar=tap, in1=acc[:],
                                                                 op0=ALU.mult, op1=ALU.add))
                        continue
                    dve.wait_ge(conv_free, 16 * (j + 1))
                    nc.vector.scalar_tensor_tensor(out=conv_out[:, bass.ds(j % 2, 1), :].rearrange("p o t -> p (o t)"),
                                                   in0=src, scalar=tap, in1=acc[:], op0=ALU.mult,
                                                   op1=ALU.add).then_inc(conv_ok, 1)

        @block.tensor
        def _(pe):
            def transposes(n, r):
                pe.wait_ge(h_ok, RB * n + (r + 1))
                for k in range(KT):
                    last = nc.tensor.transpose(tp[r % 2][:, k, :], xs[:, r, bass.ts(k, P)], ident[:])
                last.then_inc(tp_ok, 1)

            def products(slot, ks, rhs_at, bank, done):
                for k in ks:
                    for w, h in ((w_hi, hT_hi), (w_hi, hT_lo), (w_lo, hT_hi)):
                        last = nc.tensor.matmul(mm[bank][:], w[:, slot, k, :], h[:, k, rhs_at],
                                                start=(k == 0 and w is w_hi and h is hT_hi),
                                                stop=(k == KT - 1 and w is w_lo))
                if done:
                    last.then_inc(mm_ok, 1)

            def sweep(n, m, half):
                if half == 0:
                    pe.wait_ge(mm_free, 2 * n + (m + 1))
                products(m, range(half * KT // 2, (half + 1) * KT // 2), bass.ds(n * BLK, BLK), 2 + m, half == 1)

            pe.wait_ge(con_ld, 16)
            for r in range(RB):
                if r >= 2:
                    pe.wait_ge(lo_ok, r - 1)
                transposes(0, r)
            pe.wait_ge(wlo_ok, 2)
            with pe.Fori(1, NB) as n:
                pe.wait_ge(lo_ok, RB * n)
                for r in range(RB):
                    pe.wait_ge(lo_ok, RB * n + (r - 1))
                    transposes(n, r)
                    sweep(n - 1, r // 2, r % 2)
            pe.wait_ge(lo_ok, NT)
            for m in range(2):
                for half in range(2):
                    sweep(NB - 1, m, half)

            with pe.Fori(0, CT - 1) as j:
                for u in range(4):
                    pe.wait_ge(wlo_ok, 4 * j + (u + 3))
                    for n in range(NB):
                        pe.wait_ge(mm_free, 4 * NB * j + (2 * NB + NB * u + n - 1))
                        products(u % 2, range(KT), bass.ts(n, BLK), n, True)


class Tile:

    def __init__(self, i, k):
        self.t, self.slot, self.nth = 2 * i + k, k % 2, i + k // 2

    def tokens(self):
        return bass.ts(self.t, P) if isinstance(self.t, int) else bass.ds(self.t * P, P)


def after(eng, sem, value):
    if not isinstance(value, int) or value > 0:
        eng.wait_ge(sem, value)


def each(ap, n):
    return ap.unsqueeze(1).broadcast_to([P, n, ap.shape[1]])


def along(ap, n):
    return ap.unsqueeze(2).broadcast_to([P, ap.shape[1], n])


TWO_PI = 2 * np.pi
PI_1 = 6.28125
PI_2 = float(np.float32(round((TWO_PI - PI_1) * 2 ** 17) / 2 ** 17))
PI_3 = float(np.float32(TWO_PI - PI_1 - PI_2))
ROUND = 1.5 * 2.0 ** 23
BELOW_PI = 3.1415925
MASKED = -3.0e38
SCALE = HEAD ** -0.5
CHUNKS = P // CHUNK
GROUPS = 4
KEYS = 2 * CHUNK


def phase_mix(nc, positions, par, con, w_o, ln_g, ln_b, h_scr, qkv_scr, conv_scr, h1_scr, h1T_scr):
    ctx = ExitStack()
    with ctx:
        def sb(name, shape, dt=F32):
            return ctx.enter_context(nc.sbuf_tensor(name, shape, dt))

        def ps(name, shape):
            return ctx.enter_context(nc.psum_tensor(name, shape, F32))

        def sem(name):
            return ctx.enter_context(nc.semaphore(name))

        wo_hi = sb("m_wo_hi", [P, KT, D], F32R)
        wo_lo = sb("m_wo_lo", [P, KT, D], F32R)
        mix_hi = sb("m_mix_hi", [P, 2, KT, P], F32R)
        mix_lo = sb("m_mix_lo", [P, 2, KT, P], F32R)
        ident, rot, ones = sb("m_ident", [P, P]), sb("m_rot", [P, P]), sb("m_ones", [P, P])
        freq, eps, half_pi = sb("m_freq", [P, 4]), sb("m_eps", [P, 1]), sb("m_half_pi", [P, 1])
        cg, cb, sink = sb("m_cg", [P, CT]), sb("m_cb", [P, CT]), sb("m_sink", [P, NKV, GROUPS])
        g_bc, b_bc = sb("m_g", [P, D]), sb("m_b", [P, D])
        cos, sin = sb("m_cos", [P, SEQ]), sb("m_sin", [P, SEQ])
        pos = sb("m_pos", [P, SEQ], I32)
        ang, turns = sb("m_ang", [P, SEQ]), sb("m_turns", [P, SEQ])
        qk_in = sb("m_qk_in", [P, 2, 5, P])
        v_in = sb("m_v_in", [P, 2, CHUNK + P])
        conv_in = sb("m_conv_in", [P, 2, CT, P])
        h_in = sb("m_h_in", [P, 2, D])
        qk_cos, qk_sin = sb("m_qk_cos", [P, 5, P]), sb("m_qk_sin", [P, 5, P])
        qr, kr = sb("m_qr", [P, CHUNKS, 4 * CHUNK]), sb("m_kr", [P, CHUNK + P])
        vw = sb("m_vw", [P, CHUNKS, P])
        prob = sb("m_prob", [P, NKV, GROUPS, KEYS + 1])
        top, peak = sb("m_top", [P, NKV, GROUPS]), sb("m_peak", [P, NKV, GROUPS])
        den, inv = sb("m_den", [P, NKV, GROUPS]), sb("m_inv", [P, NKV, GROUPS])
        probT = sb("m_probT", [P, NKV, BLK])
        cc, cz, ce = sb("m_cc", [P, CT, P]), sb("m_cz", [P, CT, P]), sb("m_ce", [P, CT, P])
        cv, cy, ct, cr = (sb(f"m_c{k}", [P, P]) for k in range(4))
        r = sb("m_r", [P, 2, D])
        h1T = sb("m_h1T", [P, 2, KT, P])
        stat, mv = sb("m_stat", [P, 2, 6]), sb("m_mv", [P, 2])
        lv, ly, lt, lr = (sb(f"m_l{k}", [P, 1]) for k in range(4))

        y = ps("m_y", [P, D])
        rq = ps("m_rq", [P, 4, P])
        aux = ps("m_aux", [P, BLK])
        score = [ps(f"m_score{g}", [P, GROUPS, KEYS]) for g in range(NKV)]
        tps = ps("m_tps", [P, 2 * BLK])
        mean = var = aux[:, 0:P]
        rk = aux[:, P:2 * P]
        vT = tps[:, BLK:BLK + 2 * P].rearrange("p (c k) -> p c k", c=CHUNKS)
        pv = score[0][:, :, :].rearrange("p g k -> p (g k)").rearrange("p (c t q) -> p c t q", c=CHUNKS, t=4)

        con_ld, pos_ld, row_ld = sem("m_con_ld"), sem("m_pos_ld"), sem("m_row_ld")
        wo_ld = [sem(f"m_wo_ld{s}") for s in range(2)]
        in_ld = [sem(f"m_in_ld{s}") for s in range(2)]
        h_ld = [sem(f"m_h_ld{s}") for s in range(2)]
        h1_st = [sem(f"m_h1_st{s}") for s in range(2)]
        h1T_st = [sem(f"m_h1T_st{s}") for s in range(2)]
        wo_hi_ok, wo_lo_ok, pads_ok = sem("m_wo_hi"), sem("m_wo_lo"), sem("m_pads")
        ang_seq, ang_ok, sin_ok, turn_ok = sem("m_ang"), sem("m_ang_ok"), sem("m_sin_ok"), sem("m_turn_ok")
        rq_ps, rk_ps, mean_ps, var_ps, vT_ps = (sem("m_" + n) for n in ("rq_ps", "rk_ps", "mean_ps", "var_ps", "vT_ps"))
        score_ps, probT_ps, pv_ps, y_ps, h1T_ps = (sem("m_" + n) for n in ("score_ps", "probT_ps", "pv_ps", "y_ps", "h1T_ps"))
        cos_ok, kcopy_ok, sin_qk_ok, qr_ok, kr_ok = (sem("m_" + n) for n in ("cos", "kcopy", "sin_qk", "qr", "kr"))
        centre_ok, square_ok, cy_ok, cn_ok, gate_ok, swish_ok = (sem("m_" + n) for n in ("centre", "square", "cy", "cn", "gate", "swish"))
        conv_hi_ok, conv_lo_ok, attn_hi_ok, attn_lo_ok = (sem("m_" + n) for n in ("conv_hi", "conv_lo", "attn_hi", "attn_lo"))
        vw_ok, shift_ok, exp_ok, prob_ok, probT_ok = (sem("m_" + n) for n in ("vw", "shift", "exp", "prob", "probT"))
        resid_ok, lv_ok, ly_ok, norm_ok, scaled_ok, h1_ok, h1T_ok = (sem("m_" + n) for n in ("resid", "lv", "ly", "norm", "scaled", "h1", "h1T"))
        soft_seq, cn_seq, ln_seq, z_seq, lact_seq, cact_seq, stats_seen = (sem("m_" + n) for n in ("soft_seq", "cn_seq", "ln_seq", "z_seq", "lact_seq", "cact_seq", "stats_seen"))
        block = ctx.enter_context(nc.Block())

        q_rows = qkv_scr.rearrange("q p t -> (q p) t")

        def steps(eng, first, step, last, final):
            first(Tile(0, 0))
            step(None, Tile(0, 0), Tile(0, 1))
            with eng.Fori(0, NT // 2 - 1) as i:
                step(Tile(i, 0), Tile(i, 1), Tile(i, 2))
                step(Tile(i, 1), Tile(i, 2), Tile(i, 3))
            last(Tile(NT // 2 - 1, 0), Tile(NT // 2 - 1, 1))
            final(Tile(NT // 2 - 1, 1))

        @block.sync
        def _(sp):
            sp.dma_start(pos[:], positions[0:1, :].broadcast_to([P, SEQ])).then_inc(pos_ld, 16)
            for dst, at, n in ((ident, CON_ID, P), (rot, CON_ROT, P), (ones, CON_ONES, P), (freq, CON_FREQ, 4)):
                sp.dma_start(dst[:], con[:, at:at + n]).then_inc(con_ld, 16)
            for dst, at in ((cg[:], PAR_LNG), (cb[:], PAR_LNB)):
                sp.dma_start(dst, par[:, at:at + CT]).then_inc(con_ld, 16)
            sp.dma_start(sink[:, :, :], par[:, PAR_SINK:PAR_N].rearrange("p (g a) -> p g a", g=NKV)).then_inc(con_ld, 16)

            def load_in(x):
                if isinstance(x.t, int) and x.t == 0:
                    v, at, n = v_in[:, 0, CHUNK:], 0, P
                else:
                    v, at, n = v_in[:, x.slot, :], x.t * P - CHUNK, P + CHUNK
                for g in range(NKV):
                    src = q_rows[4 * HEAD * g:4 * HEAD * (g + 1), x.tokens()].rearrange("(h d) t -> d h t", d=HEAD)
                    sp.dma_start(qk_in[HEAD * g:HEAD * (g + 1), x.slot, 0:4, :], src).then_inc(in_ld[x.slot], 16)
                sp.dma_start(qk_in[:, x.slot, 4, :], qkv_scr[4, :, x.tokens()]).then_inc(in_ld[x.slot], 16)
                sp.dma_start(v, qkv_scr[5, :, bass.ds(at, n)]).then_inc(in_ld[x.slot], 16)
                sp.dma_start(conv_in[:, x.slot, :, :], conv_scr[:, :, x.tokens()].rearrange("c p t -> p c t")).then_inc(in_ld[x.slot], 16)

            def load_h(x):
                sp.dma_start(h_in[:, x.slot, :], h_scr[bass.ds(x.t, 1), :, :].rearrange("o p d -> p (o d)")).then_inc(h_ld[x.slot], 16)

            def next_in(c, m):
                after(sp, qr_ok, c.t + 1)
                after(sp, kr_ok, c.t + 1)
                after(sp, vT_ps, c.t + 1)
                after(sp, centre_ok, c.t + 1)
                load_in(m)

            def load_wo(k):
                if k >= 2:
                    sp.wait_ge(wo_lo_ok, k - 1)
                sp.dma_start(r[:, k % 2, :], w_o[:, k, :]).then_inc(wo_ld[k % 2], 16)

            sp.wait_ge(pads_ok, 4)
            load_in(Tile(0, 0))
            load_in(Tile(0, 1))
            load_wo(0)
            load_wo(1)
            load_h(Tile(0, 0))
            sp.dma_start(g_bc[:], row_to_all(ln_g)).then_inc(row_ld, 16)
            sp.dma_start(b_bc[:], row_to_all(ln_b)).then_inc(row_ld, 16)
            for k in range(2, KT):
                load_wo(k)

            def step(p, c, n):
                if p is not None:
                    next_in(p, n)
                    sp.wait_ge(resid_ok, p.t + 1)
                load_h(n)

            steps(sp, lambda n: None, step, lambda p, c: None, lambda p: None)

        @block.gpsimd
        def _(pool):
            nc.gpsimd.memset(kr[:, P:P + CHUNK], 0.0).then_inc(pads_ok, 1)
            nc.gpsimd.memset(v_in[:, 0, 0:CHUNK], 0.0).then_inc(pads_ok, 1)
            nc.gpsimd.memset(eps[:], EPS).then_inc(pads_ok, 1)
            nc.gpsimd.memset(half_pi[:], float(np.pi / 2)).then_inc(pads_ok, 1)

            for s in range(2):
                pool.sem_inc(h1_st[s], 16)
                pool.sem_inc(h1T_st[s], 16)

            def rotate(n):
                pool.wait_ge(in_ld[n.slot], n.nth * 80 + 80)
                after(pool, score_ps, NKV * n.t)
                tok = n.tokens()
                nc.gpsimd.tensor_tensor(qk_cos[:, :, :], qk_in[:, n.slot, :, :], each(cos[:, tok], 5), ALU.mult).then_inc(cos_ok, 1)
                nc.gpsimd.tensor_copy(kr[:, 0:CHUNK], kr[:, P:P + CHUNK]).then_inc(kcopy_ok, 1)
                pool.wait_ge(cos_ok, n.t + 1)
                pool.wait_ge(kcopy_ok, n.t + 1)
                pool.wait_ge(sin_qk_ok, 2 * n.t + 1)
                nc.gpsimd.tensor_tensor(kr[:, CHUNK:], qk_cos[:, 4, :], qk_sin[:, 4, :], ALU.add).then_inc(kr_ok, 1)
                pool.wait_ge(sin_qk_ok, 2 * n.t + 2)
                view = "p t (c q) -> p c t q"
                nc.gpsimd.tensor_tensor(qr[:, :, :].rearrange("p c (t q) -> p c t q", t=4),
                                        qk_cos[:, 0:4, :].rearrange(view, c=CHUNKS),
                                        qk_sin[:, 0:4, :].rearrange(view, c=CHUNKS), ALU.add).then_inc(qr_ok, 1)

            def affine(p):
                pool.wait_ge(norm_ok, p.t + 1)
                nc.gpsimd.tensor_tensor(r[:, p.slot, :], r[:, p.slot, :], g_bc[:], ALU.mult).then_inc(scaled_ok, 1)
                pool.wait_ge(scaled_ok, p.t + 1)
                nc.gpsimd.tensor_tensor(r[:, p.slot, :], r[:, p.slot, :], b_bc[:], ALU.add).then_inc(h1_ok, 1)

            def step(p, c, n):
                rotate(n)
                if p is not None:
                    affine(p)

            pool.wait_ge(sin_ok, 2)
            pool.wait_ge(row_ld, 32)
            pool.wait_ge(pads_ok, 4)
            steps(pool, rotate, step, lambda p, c: affine(p), affine)

        @block.scalar
        def _(act):
            act.wait_ge(pads_ok, 4)
            act.wait_ge(ang_ok, 1)
            nc.scalar.activation(sin[:], ang[:], ACT.Sin).then_inc(sin_ok, 1)
            act.wait_ge(ang_ok, 2)
            nc.scalar.activation(cos[:], turns[:], ACT.Sin, bias=half_pi[:], scale=-1.0).then_inc(sin_ok, 1)
            nc.scalar.preload_act_table_set("natural_log_exp_and_others")
            for k in range(KT):
                act.wait_ge(wo_ld[k % 2], 16 * (k // 2 + 1))
                nc.scalar.copy(wo_hi[:, k, :], r[:, k % 2, :]).then_inc(wo_hi_ok, 1)

            def attn_hi(c):
                act.wait_ge(pv_ps, c.t + 1)
                nc.scalar.copy(mix_hi[:, c.slot, 0:4, :].rearrange("p t (c q) -> p c t q", c=CHUNKS), pv).then_inc(attn_hi_ok, 1)

            def square(n):
                act.wait_ge(centre_ok, n.t + 1)
                nc.scalar.activation(cz[:, :, :], cc[:, :, :], ACT.Square).then_inc(square_ok, 1)

            def exps(n, g):
                act.wait_ge(shift_ok, NKV * n.t + (g + 1))
                nc.scalar.activation(prob[:, g, :, :], prob[:, g, :, :], ACT.Exp).then_inc(exp_ok, 1)

            def conv_root(n):
                act.wait_ge(var_ps, n.t + 1)
                nc.scalar.activation(ce[:, 0, :], var, ACT.Ln, bias=eps[:]).then_inc(cact_seq, 1)
                act.wait_ge(cact_seq, 2 * n.t + 1)
                nc.scalar.activation(cy[:], ce[:, 0, :], ACT.Exp, scale=-0.5).then_inc(cy_ok, 1)

            def gates(n):
                act.wait_ge(cn_ok, n.t + 1)
                for j in range(CT):
                    last = nc.scalar.activation(cz[:, j, :], cc[:, j, :], ACT.Identity, bias=cb[:, j:j + 1], scale=cg[:, j:j + 1])
                last.then_inc(cact_seq, 1)
                act.wait_ge(cact_seq, 2 * n.t + 2)
                nc.scalar.activation(ce[:, :, :], cz[:, :, :], ACT.Exp, scale=-1.0).then_inc(gate_ok, 1)

            def conv_hi(n):
                act.wait_ge(swish_ok, n.t + 1)
                nc.scalar.copy(mix_hi[:, n.slot, 4:8, :], cc[:, :, :]).then_inc(conv_hi_ok, 1)

            def row_root(p):
                act.wait_ge(lv_ok, p.t + 1)
                nc.scalar.activation(lt[:], lv[:], ACT.Ln).then_inc(lact_seq, 1)
                act.wait_ge(lact_seq, p.t + 1)
                nc.scalar.activation(ly[:], lt[:], ACT.Exp, scale=-0.5).then_inc(ly_ok, 1)

            def out_T(p):
                act.wait_ge(h1T_ps, p.t + 1)
                act.wait_ge(h1T_st[p.slot], 16 * p.nth + 16)
                nc.scalar.copy(h1T[:, p.slot, :, :], tps[:].rearrange("p (k t) -> p k t", k=KT)).then_inc(h1T_ok, 1)

            def store(p):
                act.wait_ge(h1_ok, p.t + 1)
                act.dma_start(h1_scr[bass.ds(p.t, 1), :, :].rearrange("o p d -> p (o d)"), r[:, p.slot, :]).then_inc(h1_st[p.slot], 16)
                act.wait_ge(h1T_ok, p.t + 1)
                act.dma_start(h1T_scr[:, :, p.tokens()].rearrange("k p t -> p k t"), h1T[:, p.slot, :, :]).then_inc(h1T_st[p.slot], 16)

            def probs_T(n):
                for g in range(NKV):
                    act.wait_ge(probT_ps, NKV * n.t + (g + 1))
                    nc.scalar.copy(probT[:, g, :], tps[:, g * BLK:(g + 1) * BLK]).then_inc(probT_ok, 1)

            def step(p, c, n):
                if c is not None:
                    attn_hi(c)
                square(n)
                if p is not None:
                    row_root(p)
                exps(n, 0)
                conv_root(n)
                exps(n, 1)
                gates(n)
                if p is not None:
                    out_T(p)
                conv_hi(n)
                probs_T(n)
                if p is not None:
                    store(p)

            def last(p, c):
                attn_hi(c)
                row_root(p)
                out_T(p)
                store(p)

            def final(p):
                row_root(p)
                out_T(p)
                store(p)
                for s in range(2):
                    act.wait_ge(h1_st[s], 16 * (NT // 2 + 1))
                    act.wait_ge(h1T_st[s], 16 * (NT // 2 + 1))

            steps(act, lambda n: step(None, None, n), step, last, final)

        @block.vector
        def _(dve):
            seq = Count(ang_seq, dve)
            dve.wait_ge(pos_ld, 16)
            dve.wait_ge(con_ld, 16 * 7)
            seq.inc(nc.vector.tensor_copy(ang[:], pos[:]))
            seq.wait()
            seq.inc(nc.vector.tensor_scalar(ang[:], ang[:], freq[:, 0:1], None, ALU.mult))
            seq.wait()
            seq.inc(nc.vector.tensor_scalar(turns[:], ang[:], 1 / TWO_PI, ROUND, ALU.mult, ALU.add))
            seq.wait()
            seq.inc(nc.vector.tensor_scalar(turns[:], turns[:], ROUND, None, ALU.subtract))
            for part in (PI_1, PI_2, PI_3):
                seq.wait()
                seq.inc(nc.vector.scalar_tensor_tensor(out=ang[:], in0=turns[:], scalar=-part, in1=ang[:], op0=ALU.mult, op1=ALU.add))
            seq.wait()
            nc.vector.tensor_scalar(ang[:], ang[:], BELOW_PI, -BELOW_PI, ALU.min, ALU.max).then_inc(ang_ok, 1)
            dve.wait_ge(ang_ok, 1)
            nc.vector.scalar_tensor_tensor(out=turns[:], in0=ang[:], scalar=-1.0, in1=ang[:], op0=ALU.mult, op1=ALU.max).then_inc(ang_ok, 1)
            for k in range(KT):
                dve.wait_ge(wo_hi_ok, k + 1)
                nc.vector.tensor_tensor(wo_lo[:, k, :], r[:, k % 2, :], wo_hi[:, k, :].bitcast(F32), ALU.subtract).then_inc(wo_lo_ok, 1)

            def residual(p):
                dve.wait_ge(y_ps, p.t + 1)
                dve.wait_ge(h_ld[p.slot], 16 * p.nth + 16)
                dve.wait_ge(h1_st[p.slot], 16 * p.nth + 16)
                nc.vector.scalar_tensor_tensor(out=r[:, p.slot, :], in0=h_in[:, p.slot, :], scalar=ALPHA, in1=y[:],
                                               op0=ALU.mult, op1=ALU.add).then_inc(resid_ok, 1)

            def attn_lo(c):
                dve.wait_ge(attn_hi_ok, c.t + 1)
                view = "p t (c q) -> p c t q"
                nc.vector.tensor_tensor(mix_lo[:, c.slot, 0:4, :].rearrange(view, c=CHUNKS), pv,
                                        mix_hi[:, c.slot, 0:4, :].bitcast(F32).rearrange(view, c=CHUNKS),
                                        ALU.subtract).then_inc(attn_lo_ok, 1)

            def rotate(n):
                tok = n.tokens()
                after(dve, qr_ok, n.t)
                dve.wait_ge(rk_ps, n.t + 1)
                nc.vector.tensor_tensor(qk_sin[:, 4, :], rk, sin[:, tok], ALU.mult).then_inc(sin_qk_ok, 1)
                dve.wait_ge(rq_ps, n.t + 1)
                nc.vector.tensor_tensor(qk_sin[:, 0:4, :], rq[:, :, :], each(sin[:, tok], 4), ALU.mult).then_inc(sin_qk_ok, 1)

            def centre(n):
                dve.wait_ge(mean_ps, n.t + 1)
                after(dve, conv_lo_ok, n.t)
                nc.vector.tensor_tensor(cc[:, :, :], conv_in[:, n.slot, :, :], each(mean, CT), ALU.subtract).then_inc(centre_ok, 1)

            def row_stats(p):
                seq = Count(ln_seq, dve)
                seq.base = p.t * 6
                dve.wait_ge(resid_ok, p.t + 1)
                for a in range(2):
                    seq.inc(nc.vector.bn_stats(stat[:, a, :], r[:, p.slot, a * BLK:(a + 1) * BLK]))
                seq.wait()
                dve.sem_inc(stats_seen, 1)
                seq.inc(nc.vector.bn_aggr(mv[:], stat[:].rearrange("p a s -> p (a s)")))
                seq.wait()
                nc.vector.tensor_scalar(lv[:], mv[:, 1:2], EPS, None, ALU.add).then_inc(lv_ok, 1)

            def row_norm(p):
                seq = Count(ln_seq, dve)
                seq.base, seq.n = p.t * 6, 3
                dve.wait_ge(ly_ok, p.t + 1)
                refine_rstd(nc, seq, lr[:], lv[:], ly[:], lt[:])
                seq.wait()
                nc.vector.tensor_scalar(r[:, p.slot, :], r[:, p.slot, :], mv[:, 0:1], lr[:], ALU.subtract, ALU.mult).then_inc(norm_ok, 1)
                assert seq.n == 6

            def soft_at(n, g, k):
                return n.t * (NKV * 5) + (3 * g + k)

            def soft_shift(n, g):
                dve.wait_ge(score_ps, NKV * n.t + (g + 1))
                if isinstance(n.t, int) and n.t == 0:
                    nc.vector.memset(score[g][:, 0:2, 0:CHUNK], MASKED).then_inc(pads_ok, 1)
                    dve.wait_ge(pads_ok, 5 + g)
                nc.vector.tensor_reduce(top[:, g, :], score[g][:, :, :], AX.X, ALU.max).then_inc(soft_seq, 1)
                dve.wait_ge(soft_seq, soft_at(n, g, 1))
                nc.vector.scalar_tensor_tensor(out=peak[:, g, :], in0=top[:, g, :], scalar=SCALE, in1=sink[:, g, :], op0=ALU.mult,
                                               op1=ALU.max).then_inc(soft_seq, 1)
                dve.wait_ge(soft_seq, soft_at(n, g, 2))
                after(dve, probT_ps, NKV * n.t)
                nc.vector.tensor_tensor(prob[:, g, :, KEYS], sink[:, g, :], peak[:, g, :], ALU.subtract).then_inc(soft_seq, 1)
                nc.vector.scalar_tensor_tensor(out=prob[:, g, :, 0:KEYS], in0=score[g][:, :, :], scalar=SCALE,
                                               in1=along(peak[:, g, :], KEYS), op0=ALU.mult, op1=ALU.subtract).then_inc(shift_ok, 1)

            def soft_norm(n, g):
                dve.wait_ge(exp_ok, NKV * n.t + (g + 1))
                nc.vector.tensor_reduce(den[:, g, :], prob[:, g, :, :], AX.X, ALU.add).then_inc(soft_seq, 1)
                dve.wait_ge(soft_seq, n.t * (NKV * 5) + (3 * NKV + 2 * g + 1))
                nc.vector.reciprocal(inv[:, g, :], den[:, g, :]).then_inc(soft_seq, 1)
                dve.wait_ge(soft_seq, n.t * (NKV * 5) + (3 * NKV + 2 * g + 2))
                nc.vector.tensor_tensor(prob[:, g, :, 0:KEYS], prob[:, g, :, 0:KEYS], along(inv[:, g, :], KEYS), ALU.mult).then_inc(prob_ok, 1)

            def take_v(n):
                dve.wait_ge(vT_ps, n.t + 1)
                after(dve, pv_ps, n.t)
                nc.vector.tensor_copy(vw[:, :, :], vT).then_inc(vw_ok, 1)

            def conv_norm(n):
                seq = Count(cn_seq, dve)
                seq.base = n.t * 4
                dve.wait_ge(cy_ok, n.t + 1)
                seq.inc(nc.vector.tensor_scalar(cv[:], var, EPS, None, ALU.add))
                refine_rstd(nc, seq, cr[:], cv[:], cy[:], ct[:])
                seq.wait()
                assert seq.n == 4
                nc.vector.tensor_tensor(cc[:, :, :], cc[:, :, :], each(cr[:], CT), ALU.mult).then_inc(cn_ok, 1)

            def swish(n):
                dve.wait_ge(gate_ok, n.t + 1)
                nc.vector.tensor_scalar(ce[:, :, :], ce[:, :, :], 1.0, None, ALU.add).then_inc(z_seq, 1)
                dve.wait_ge(z_seq, 2 * n.t + 1)
                nc.vector.reciprocal(ce[:, :, :], ce[:, :, :]).then_inc(z_seq, 1)
                dve.wait_ge(z_seq, 2 * n.t + 2)
                nc.vector.tensor_tensor(cc[:, :, :], cz[:, :, :], ce[:, :, :], ALU.mult).then_inc(swish_ok, 1)
                dve.wait_ge(conv_hi_ok, n.t + 1)
                nc.vector.tensor_tensor(mix_lo[:, n.slot, 4:8, :], cc[:, :, :], mix_hi[:, n.slot, 4:8, :].bitcast(F32),
                                        ALU.subtract).then_inc(conv_lo_ok, 1)

            def step(p, c, n):
                if p is not None:
                    residual(p)
                if c is not None:
                    attn_lo(c)
                rotate(n)
                centre(n)
                if p is not None:
                    row_stats(p)
                soft_shift(n, 0)
                if p is not None:
                    row_norm(p)
                soft_shift(n, 1)
                take_v(n)
                conv_norm(n)
                soft_norm(n, 0)
                soft_norm(n, 1)
                swish(n)

            def last(p, c):
                residual(p)
                attn_lo(c)
                row_stats(p)
                row_norm(p)

            def final(p):
                residual(p)
                row_stats(p)
                row_norm(p)

            steps(dve, lambda n: step(None, None, n), step, last, final)

        @block.tensor
        def _(pe):
            pe.wait_ge(con_ld, 16 * 7)
            pe.wait_ge(pads_ok, 4)

            def rotate_and_mean(n):
                pe.wait_ge(in_ld[n.slot], n.nth * 80 + 80)
                after(pe, cn_ok, n.t)
                after(pe, sin_qk_ok, 2 * n.t)
                nc.tensor.matmul(rk, rot[:], qk_in[:, n.slot, 4, :], start=True, stop=True).then_inc(rk_ps, 1)
                nc.tensor.matmul(rq[:, :, :], rot[:], qk_in[:, n.slot, 0:4, :], start=True, stop=True).then_inc(rq_ps, 1)
                pe.wait_ge(sin_qk_ok, 2 * n.t + 1)
                for j in range(CT):
                    m = nc.tensor.matmul(mean, ones[:], conv_in[:, n.slot, j, :], start=j == 0, stop=j == CT - 1)
                m.then_inc(mean_ps, 1)

            def scores(n):
                pe.wait_ge(kr_ok, n.t + 1)
                pe.wait_ge(qr_ok, n.t + 1)
                after(pe, attn_lo_ok, n.t)
                after(pe, shift_ok, NKV * n.t)
                for g in range(NKV):
                    at = slice(HEAD * g, HEAD * (g + 1))
                    for c in range(CHUNKS):
                        for a in range(2):
                            m = nc.tensor.matmul(score[g][:, 2 * c + a, :], qr[at, c, 2 * CHUNK * a:2 * CHUNK * (a + 1)],
                                                 kr[at, CHUNK * c:CHUNK * c + KEYS], start=True, stop=True)
                    m.then_inc(score_ps, 1)

            def variance_and_values(n):
                pe.wait_ge(centre_ok, n.t + 1)
                pe.wait_ge(square_ok, n.t + 1)
                for j in range(CT):
                    m = nc.tensor.matmul(var, ones[:], cz[:, j, :], start=j == 0, stop=j == CT - 1)
                m.then_inc(var_ps, 1)
                after(pe, probT_ok, NKV * n.t)
                for c in range(CHUNKS):
                    m = nc.tensor.transpose(vT[:, c, :], v_in[:, n.slot, CHUNK * c:CHUNK * c + KEYS], ident[:])
                m.then_inc(vT_ps, 1)

            def project(c, ks):
                for k in ks:
                    if k == 4:
                        pe.wait_ge(conv_lo_ok, c.t + 1)
                        after(pe, resid_ok, c.t)
                    if k == 0:
                        pe.wait_ge(attn_lo_ok, c.t + 1)
                    for a, w in ((mix_hi, wo_hi), (mix_hi, wo_lo), (mix_lo, wo_hi)):
                        for half in range(2):
                            at = slice(half * BLK, (half + 1) * BLK)
                            m = nc.tensor.matmul(y[:, at], a[:, c.slot, k, :], w[:, k, at],
                                                 start=(k == 4 and w is wo_hi and a is mix_hi),
                                                 stop=(k == 3 and a is mix_lo))
                if ks[-1] == 3:
                    m.then_inc(y_ps, 1)

            def h1_transposes(p):
                pe.wait_ge(h1_ok, p.t + 1)
                after(pe, probT_ok, NKV * (p.t + 2))
                for k in range(KT):
                    m = nc.tensor.transpose(tps[:, k * P:(k + 1) * P], r[:, p.slot, k * P:(k + 1) * P], ident[:])
                m.then_inc(h1T_ps, 1)

            def prob_transposes(n):
                after(pe, h1T_ok, n.t - 1)
                for b in range(NKV):
                    pe.wait_ge(prob_ok, NKV * n.t + (b + 1))
                    for g in range(GROUPS):
                        m = nc.tensor.transpose(tps[:, b * BLK + g * P:b * BLK + (g + 1) * P], prob[:, b, g, 0:KEYS], ident[:])
                    m.then_inc(probT_ps, 1)

            def values(n):
                for g in range(NKV):
                    pe.wait_ge(probT_ok, NKV * n.t + (g + 1))
                    for c in range(CHUNKS):
                        m = nc.tensor.matmul(pv[HEAD * g:HEAD * (g + 1), c, :, :], vw[:, c, HEAD * g:HEAD * (g + 1)],
                                             probT[:, g, 2 * P * c:2 * P * (c + 1)], start=True, stop=True)
                m.then_inc(pv_ps, 1)

            def step(p, c, n):
                rotate_and_mean(n)
                if c is not None:
                    project(c, (4, 5, 6))
                scores(n)
                variance_and_values(n)
                if c is not None:
                    project(c, (7, 0, 1))
                pe.wait_ge(vw_ok, n.t + 1)
                if p is not None:
                    h1_transposes(p)
                if c is not None:
                    project(c, (2,))
                prob_transposes(n)
                if c is not None:
                    project(c, (3,))
                values(n)

            def last(p, c):
                project(c, (4, 5, 6, 7, 0, 1, 2, 3))
                h1_transposes(p)

            def first(n):
                step(None, None, n)
                pe.wait_ge(wo_lo_ok, KT)

            def final(p):
                pe.wait_ge(h1_ok, p.t + 1)
                pe.wait_ge(h1T_ok, p.t)
                for k in range(KT):
                    m = nc.tensor.transpose(tps[:, k * P:(k + 1) * P], r[:, p.slot, k * P:(k + 1) * P], ident[:])
                m.then_inc(h1T_ps, 1)

            steps(pe, first, step, last, final)


def phase_up(nc, par, w_tiles, h1T_scr, act_scr):
    ctx = ExitStack()
    with ctx:
        def sb(name, shape, dt=F32):
            return ctx.enter_context(nc.sbuf_tensor(name, shape, dt))

        def sem(name):
            return ctx.enter_context(nc.semaphore(name))

        hT_hi = sb("u_hT_hi", [P, KT, SEQ], F32R)
        hT_lo = sb("u_hT_lo", [P, KT, SEQ], F32R)
        w_raw = sb("u_w_raw", [P, 2, KT, P])
        w_hi = sb("u_w_hi", [P, 2, KT, P], F32R)
        w_lo = sb("u_w_lo", [P, 2, KT, P], F32R)
        PAD = FTAPS - 1
        z = sb("u_z", [P, 2, PAD + SEQ])
        y = sb("u_y", [P, 2, SEQ])
        stage = y[:, :, :].rearrange("p s (k t) -> p s k t", k=KT // 2)
        taps = sb("u_taps", [P, 2 * FT, FTAPS])
        bias = sb("u_bias", [P, 2 * FT])
        mm = [[ctx.enter_context(nc.psum_tensor(f"u_mm{m}{n}", [P, BLK], F32)) for n in range(NB)] for m in range(2)]

        par_ld = sem("u_par_ld")
        w_ld = [sem(f"u_w_ld{s}") for s in range(2)]
        h_ld = [sem(f"u_h_ld{s}") for s in range(2)]
        hi_ok, lo_ok, whi_ok, wlo_ok = sem("u_hi"), sem("u_lo"), sem("u_whi"), sem("u_wlo")
        mm_ok, z_ok, pad_ok, conv_seq, conv_ok = sem("u_mm"), sem("u_z_ok"), sem("u_pad"), sem("u_conv_seq"), sem("u_conv")
        gelu_ok, act_ok, act_st = sem("u_gelu"), sem("u_act"), sem("u_act_st")
        block = ctx.enter_context(nc.Block())

        def products_count(j, m, n):
            return 2 * NB * j + (NB * m + n)

        @block.sync
        def _(sp):
            for s in range(2):
                sp.dma_start(w_raw[:, s, :, :], w_tiles[s, :, :, :]).then_inc(w_ld[s], 16)
            for q in range(2 * NB):
                if q >= 2:
                    sp.wait_ge(lo_ok, q - 1)
                src = h1T_scr[(q % 2) * KT // 2:(q % 2 + 1) * KT // 2, :, bass.ts(q // 2, BLK)]
                sp.dma_start(stage[:, q % 2, :, :], src.rearrange("k p t -> p k t")).then_inc(h_ld[q % 2], 16)
                if q == 0:
                    sp.dma_start(taps[:, :, :], par[:, PAR_FTAPS:PAR_FB].rearrange("p (c t) -> p c t", t=FTAPS)).then_inc(par_ld, 16)
                    sp.dma_start(bias[:], par[:, PAR_FB:PAR_SINK]).then_inc(par_ld, 16)

            def store(j):
                sp.wait_ge(act_ok, j + 1)
                sp.dma_start(act_scr[bass.ds(j, 1), :, :].rearrange("o p t -> p (o t)"), y[:, 1, :]).then_inc(act_st, 16)

            with sp.Fori(1, FT) as j:
                for m in range(2):
                    sp.wait_ge(wlo_ok, 2 * j + (m - 1))
                    sp.dma_start(w_raw[:, m, :, :], w_tiles[bass.ds(2 * j + m, 1), :, :, :].rearrange("o p k c -> p (o k) c")).then_inc(w_ld[m], 16)
                store(j - 1)
            store(FT - 1)
            sp.wait_ge(act_st, 16 * FT)

        @block.gpsimd
        def _(pool):
            nc.gpsimd.memset(z[:, :, 0:PAD], 0.0).then_inc(pad_ok, 1)

        @block.scalar
        def _(act):
            def weights_hi(nth, slot):
                act.wait_ge(w_ld[slot], nth * 16)
                nc.scalar.copy(w_hi[:, slot, :, :], w_raw[:, slot, :, :]).then_inc(whi_ok, 1)

            def take(count, m, n):
                act.wait_ge(mm_ok, count + 1)
                nc.scalar.copy(z[:, m, bass.ds(PAD + n * BLK, BLK)], mm[m][n][:]).then_inc(z_ok, 1)

            def gelu(j):
                act.wait_ge(conv_ok, 2 * j + 1)
                nc.scalar.activation(y[:, 0, :], y[:, 0, :], ACT.Gelu).then_inc(gelu_ok, 1)

            nc.scalar.preload_act_table(ACT.Gelu)
            weights_hi(1, 0)
            weights_hi(1, 1)
            for q in range(2 * NB):
                act.wait_ge(h_ld[q % 2], 16 * (q // 2 + 1))
                at = slice((q % 2) * KT // 2, (q % 2 + 1) * KT // 2)
                nc.scalar.copy(hT_hi[:, at, bass.ts(q // 2, BLK)], stage[:, q % 2, :, :]).then_inc(hi_ok, 1)
                if q % 2 and q > 1:
                    for m in range(2):
                        take(q - 3 + m, m, q // 2 - 1)
            for m in range(2):
                take(2 * NB - 2 + m, m, NB - 1)
            weights_hi(2, 0)
            weights_hi(2, 1)
            gelu(0)

            def pair(j, last):
                act.wait_ge(conv_ok, 2 * j - 1)
                for n in range(NB):
                    take(products_count(j, 0, n), 0, n)
                if not last:
                    weights_hi(j + 2, 0)
                act.wait_ge(conv_ok, 2 * j)
                for n in range(NB):
                    take(products_count(j, 1, n), 1, n)
                    if n == 1:
                        gelu(j)
                if not last:
                    weights_hi(j + 2, 1)

            with act.Fori(1, FT - 1) as j:
                pair(j, False)
            pair(FT - 1, True)

        @block.vector
        def _(dve):
            def weights_lo(s, slot):
                dve.wait_ge(whi_ok, s + 1)
                nc.vector.tensor_tensor(w_lo[:, slot, :, :], w_raw[:, slot, :, :], w_hi[:, slot, :, :].bitcast(F32),
                                        ALU.subtract).then_inc(wlo_ok, 1)

            def tap(s, k):
                return taps[:, bass.ds(s, 1), k:k + 1].rearrange("p o t -> p (o t)")

            def convolve(j, m):
                s, steps = 2 * j + m, FTAPS - 1
                dve.wait_ge(z_ok, NB * s + NB)
                nc.vector.tensor_scalar(y[:, m, :], z[:, m, PAD:], tap(s, PAD), bias[:, bass.ds(s, 1)], ALU.mult,
                                        ALU.add).then_inc(conv_seq, 1)
                for k in range(PAD):
                    dve.wait_ge(conv_seq, steps * s + (k + 1))
                    v = nc.vector.scalar_tensor_tensor(out=y[:, m, :], in0=z[:, m, k:k + SEQ], scalar=tap(s, k),
                                                       in1=y[:, m, :], op0=ALU.mult, op1=ALU.add)
                    v.then_inc(conv_seq if k < PAD - 1 else conv_ok, 1)

            def gated(j):
                dve.wait_ge(gelu_ok, j + 1)
                dve.wait_ge(conv_ok, 2 * j + 2)
                nc.vector.tensor_tensor(y[:, 1, :], y[:, 1, :], y[:, 0, :], ALU.mult).then_inc(act_ok, 1)

            weights_lo(0, 0)
            weights_lo(1, 1)
            for q in range(2 * NB):
                dve.wait_ge(hi_ok, q + 1)
                at = slice((q % 2) * KT // 2, (q % 2 + 1) * KT // 2)
                nc.vector.tensor_tensor(hT_lo[:, at, bass.ts(q // 2, BLK)], stage[:, q % 2, :, :],
                                        hT_hi[:, at, bass.ts(q // 2, BLK)].bitcast(F32), ALU.subtract).then_inc(lo_ok, 1)
            dve.wait_ge(par_ld, 32)
            dve.wait_ge(pad_ok, 1)
            weights_lo(2, 0)
            weights_lo(3, 1)
            convolve(0, 0)
            convolve(0, 1)
            gated(0)

            def pair(j, last):
                dve.wait_ge(act_ok, j)
                convolve(j, 0)
                if not last:
                    weights_lo(2 * j + 2, 0)
                dve.wait_ge(act_st, 16 * j)
                convolve(j, 1)
                gated(j)
                if not last:
                    weights_lo(2 * j + 3, 1)

            with dve.Fori(1, FT - 1) as j:
                pair(j, False)
            pair(FT - 1, True)

        @block.tensor
        def _(pe):
            def products(m, n):
                for k in range(KT):
                    for w, h in ((w_hi, hT_hi), (w_hi, hT_lo), (w_lo, hT_hi)):
                        last = nc.tensor.matmul(mm[m][n][:], w[:, m, k, :], h[:, k, bass.ts(n, BLK)],
                                                start=(k == 0 and w is w_hi and h is hT_hi),
                                                stop=(k == KT - 1 and w is w_lo))
                last.then_inc(mm_ok, 1)

            pe.wait_ge(wlo_ok, 2)
            for n in range(NB):
                pe.wait_ge(lo_ok, 2 * n + 2)
                for m in range(2):
                    products(m, n)
            with pe.Fori(1, FT) as j:
                for m in range(2):
                    pe.wait_ge(wlo_ok, 2 * j + (m + 1))
                    for n in range(NB):
                        pe.wait_ge(z_ok, products_count(j, m, n) - 3)
                        products(m, n)


def phase_down(nc, w_down, ln_g, ln_b, act_scr, h1_scr, out):
    ctx = ExitStack()
    with ctx:
        def sb(name, shape, dt=F32):
            return ctx.enter_context(nc.sbuf_tensor(name, shape, dt))

        def sem(name):
            return ctx.enter_context(nc.semaphore(name))

        RAW = 3
        wd_hi = sb("d_wd_hi", [P, HALF, D], F32R)
        wd_lo = sb("d_wd_lo", [P, HALF, D], F32R)
        wd_raw = sb("d_wd_raw", [P, RAW, D])
        total = sb("d_total", [P, NT, D])
        a_raw = sb("d_a_raw", [P, 2, HALF, P])
        a_hi = sb("d_a_hi", [P, 2, HALF, P], F32R)
        a_lo = sb("d_a_lo", [P, 2, HALF, P], F32R)
        g_bc, b_bc = sb("d_g", [P, D]), sb("d_b", [P, D])
        stat, mv = sb("d_stat", [P, 2, 6]), sb("d_mv", [P, 2])
        lv, ls, ly, lt, lr = (sb(f"d_l{k}", [P, 1]) for k in range(5))
        y = [ctx.enter_context(nc.psum_tensor(f"d_y{s}", [P, D], F32)) for s in range(2)]

        wd_ld = [sem(f"d_wd_ld{s}") for s in range(RAW)]
        a_ld = [sem(f"d_a_ld{s}") for s in range(2)]
        row_ld, out_st = sem("d_row_ld"), sem("d_out_st")
        h1_ld = [sem(f"d_h1_ld{s}") for s in range(2)]
        whi_ok, wlo_ok, used_ok = sem("d_whi"), sem("d_wlo"), sem("d_used")
        ahi_ok, alo_ok, y_ok, sum_ok = sem("d_ahi"), sem("d_alo"), sem("d_y_ok"), sem("d_sum")
        ln_seq, lv_ok, ls_ok, norm_ok, scaled_ok, out_ok = (sem("d_" + n) for n in ("ln_seq", "lv", "ls", "norm", "scaled", "out"))
        stats_seen, pool_seen = sem("d_stats_seen"), sem("d_pool_seen")
        block = ctx.enter_context(nc.Block())

        def run(eng, step):
            for f in range(2):
                step(NT * f, 0, f, 0, NT // 2 * f + 1, "first")
                with eng.Fori(0, NT // 2 - 1) as i:
                    step(2 * i + (NT * f + 1), 2 * i + 1, f, 1, i + (NT // 2 * f + 2), "")
                    step(2 * i + (NT * f + 2), 2 * i + 2, f, 0, i + (NT // 2 * f + 2), "")
                step(NT * f + NT - 1, NT - 1, f, 1, NT // 2 * f + NT // 2 + 1, "last")

        def tile_of(t):
            return total[:, bass.ds(t, 1), :].rearrange("p o d -> p (o d)")

        def tokens(t):
            return bass.ds(t * P, P)

        @block.sync
        def _(sp):
            def load_act(t, f, slot):
                sp.dma_start(a_raw[:, slot, :, :], act_scr[HALF * f:HALF * (f + 1), :, tokens(t)].rearrange("k p t -> p k t")).then_inc(a_ld[slot], 16)

            def load_wd(k):
                if k >= RAW:
                    sp.wait_ge(wlo_ok, k - RAW + 1)
                sp.dma_start(wd_raw[:, k % RAW, :], w_down[k, :, :]).then_inc(wd_ld[k % RAW], 16)

            load_act(0, 0, 0)
            for k in range(HALF):
                load_wd(k)
            sp.dma_start(g_bc[:], row_to_all(ln_g)).then_inc(row_ld, 16)
            sp.dma_start(b_bc[:], row_to_all(ln_b)).then_inc(row_ld, 16)

            def step(u, t, f, slot, nth, at):
                if f == 0:
                    sp.dma_start(tile_of(t), h1_scr[bass.ds(t, 1), :, :].rearrange("o p d -> p (o d)")).then_inc(h1_ld[slot], 16)
                if f == 0 and at == "last":
                    sp.wait_ge(alo_ok, u)
                    load_act(0, 1, 1 - slot)
                    for k in range(HALF, 2 * HALF):
                        load_wd(k)
                elif at != "last":
                    after(sp, alo_ok, u)
                    load_act(t + 1, f, 1 - slot)
                if f == 1 and at != "first":
                    store(t - 1)

            def store(t):
                sp.wait_ge(out_ok, t + 1)
                sp.dma_start(out[0, tokens(t), :], tile_of(t)).then_inc(out_st, 16)

            run(sp, step)
            store(NT - 1)
            sp.wait_ge(out_st, 16 * NT)

        @block.gpsimd
        def _(pool):
            pool.wait_ge(row_ld, 32)
            with pool.Fori(0, NT) as t:
                pool.wait_ge(norm_ok, t + 1)
                pool.sem_inc(pool_seen, 1)
                nc.gpsimd.tensor_tensor(tile_of(t), tile_of(t), g_bc[:], ALU.mult).then_inc(scaled_ok, 1)
                pool.wait_ge(scaled_ok, t + 1)
                pool.sem_inc(pool_seen, 1)
                nc.gpsimd.tensor_tensor(tile_of(t), tile_of(t), b_bc[:], ALU.add).then_inc(out_ok, 1)

        @block.scalar
        def _(act):
            def act_hi(u, slot, nth):
                act.wait_ge(a_ld[slot], nth * 16)
                after(act, y_ok, u - 1)
                nc.scalar.copy(a_hi[:, slot, :, :], a_raw[:, slot, :, :]).then_inc(ahi_ok, 1)

            def wd_hi_of(k):
                act.wait_ge(wd_ld[k % RAW], 16 * (k // RAW + 1))
                if k >= HALF:
                    if k < 2 * HALF - 1:
                        act.wait_ge(used_ok, k - HALF + 1)
                    else:
                        act.wait_ge(y_ok, NT)
                nc.scalar.copy(wd_hi[:, k % HALF, :], wd_raw[:, k % RAW, :]).then_inc(whi_ok, 1)

            def root(t):
                act.wait_ge(lv_ok, t + 1)
                nc.scalar.activation(ls[:], lv[:], ACT.Sqrt).then_inc(ls_ok, 1)

            nc.scalar.preload_act_table(ACT.Sqrt)
            act_hi(0, 0, 1)
            for k in range(HALF):
                wd_hi_of(k)

            def step(u, t, f, slot, nth, at):
                if not (f == 1 and at == "last"):
                    act_hi(u + 1, 1 - slot, nth)
                if f == 0 and at == "last":
                    for k in range(HALF, 2 * HALF):
                        wd_hi_of(k)
                if f == 1 and at != "first":
                    root(t - 1)

            run(act, step)
            root(NT - 1)

        @block.vector
        def _(dve):
            def act_lo(u, slot):
                dve.wait_ge(ahi_ok, u + 1)
                nc.vector.tensor_tensor(a_lo[:, slot, :, :], a_raw[:, slot, :, :], a_hi[:, slot, :, :].bitcast(F32),
                                        ALU.subtract).then_inc(alo_ok, 1)

            def wd_lo_of(k):
                dve.wait_ge(whi_ok, k + 1)
                nc.vector.tensor_tensor(wd_lo[:, k % HALF, :], wd_raw[:, k % RAW, :], wd_hi[:, k % HALF, :].bitcast(F32),
                                        ALU.subtract).then_inc(wlo_ok, 1)

            def add(u, t, f, slot, uses):
                dve.wait_ge(y_ok, u + 1)
                if f == 0:
                    dve.wait_ge(h1_ld[slot], 16 * uses)
                nc.vector.scalar_tensor_tensor(out=tile_of(t), in0=tile_of(t), scalar=ALPHA if f == 0 else 1.0, in1=y[slot][:],
                                               op0=ALU.mult, op1=ALU.add).then_inc(sum_ok, 1)

            def norm(t):
                seq = Count(ln_seq, dve)
                seq.base = t * 7
                dve.wait_ge(sum_ok, t + (NT + 2))
                dve.sem_inc(stats_seen, 1)
                for a in range(2):
                    seq.inc(nc.vector.bn_stats(stat[:, a, :], tile_of(t)[:, a * BLK:(a + 1) * BLK]))
                seq.wait()
                dve.sem_inc(stats_seen, 1)
                seq.inc(nc.vector.bn_aggr(mv[:], stat[:].rearrange("p a s -> p (a s)")))
                seq.wait()
                nc.vector.tensor_scalar(lv[:], mv[:, 1:2], EPS, None, ALU.add).then_inc(lv_ok, 1)
                dve.wait_ge(ls_ok, t + 1)
                seq.inc(nc.vector.reciprocal(ly[:], ls[:]))
                refine_rstd(nc, seq, lr[:], lv[:], ly[:], lt[:])
                seq.wait()
                assert seq.n == 7
                nc.vector.tensor_scalar(tile_of(t), tile_of(t), mv[:, 0:1], lr[:], ALU.subtract, ALU.mult).then_inc(norm_ok, 1)

            dve.sem_inc(sum_ok, 1)
            act_lo(0, 0)
            for k in range(HALF):
                wd_lo_of(k)

            def step(u, t, f, slot, nth, at):
                if at == "first" and f == 1:
                    add(NT - 1, NT - 1, 0, 1 - slot, NT // 2)
                elif at != "first":
                    uses = nth - NT // 2 * f - 1
                    add(u - 1, t - 1, f, 1 - slot, uses)
                if not (f == 1 and at == "last"):
                    act_lo(u + 1, 1 - slot)
                if f == 0 and at == "last":
                    for k in range(HALF, 2 * HALF):
                        wd_lo_of(k)
                if f == 1 and at != "first":
                    norm(t - 1)

            run(dve, step)
            add(2 * NT - 1, NT - 1, 1, 1, NT // 2)
            norm(NT - 1)

        @block.tensor
        def _(pe):
            def step(u, t, f, slot, nth, at):
                pe.wait_ge(alo_ok, u + 1)
                after(pe, sum_ok, u)
                for k in range(HALF):
                    if at == "first":
                        pe.wait_ge(wlo_ok, HALF * f + k + 1)
                    for a, w in ((a_hi, wd_hi), (a_hi, wd_lo), (a_lo, wd_hi)):
                        for half in range(2):
                            cols = slice(half * BLK, (half + 1) * BLK)
                            m = nc.tensor.matmul(y[slot][:, cols], a[:, slot, k, :], w[:, k, cols],
                                                 start=(k == 0 and a is a_hi and w is wd_hi),
                                                 stop=(k == HALF - 1 and a is a_lo))
                    if f == 0 and at == "last" and k < HALF - 1:
                        m.then_inc(used_ok, 1)
                m.then_inc(y_ok, 1)

            run(pe, step)


def build(nc, io, out):
    def scratch(name, shape):
        return nc.dram_tensor(name, shape, F32, kind="Internal").ap()

    h, h1 = scratch("h_scr", (NT, P, D)), scratch("h1_scr", (NT, P, D))
    qkv, conv = scratch("qkv_scr", (QT, P, SEQ)), scratch("conv_scr", (CT, P, SEQ))
    h1T, gated = scratch("h1T_scr", (KT, P, SEQ)), scratch("gated_scr", (FT, P, SEQ))
    phase_project(nc, io["x"], io["in_ln_g"], io["in_ln_b"], io["w_in"], io["par"], io["con"], h, qkv, conv)
    phase_mix(nc, io["positions"], io["par"], io["con"], io["w_o"], io["ln1_g"], io["ln1_b"], h, qkv, conv, h1, h1T)
    phase_up(nc, io["par"], io["w_up"], h1T, gated)
    phase_down(nc, io["w_down"], io["ln2_g"], io["ln2_b"], gated, h1, out)


def lay_out(v):
    a = {k: np.asarray(w) for k, w in v.items()}

    def columns(w, tiles):
        t = w.reshape(KT, P, w.shape[1] // P, P).transpose(2, 1, 0, 3)
        return np.ascontiguousarray(t[tiles])

    def channels(w):
        return w.reshape(w.shape[0], -1, P).transpose(2, 1, 0).reshape(P, -1)

    ffn_order = [t for j in range(FT) for t in (j, FT + j)]
    ftaps = a["ffn_conv_w"][0].reshape(FTAPS, 2 * FT, P).transpose(2, 1, 0)[:, ffn_order].reshape(P, -1)
    fbias = a["ffn_conv_b"][0].reshape(2 * FT, P).T[:, ffn_order]
    pairs = np.repeat(a["sinks"][0].reshape(NKV, 2, 2), CHUNK, axis=2)
    sinks = np.tile(pairs[:, None], (1, CHUNKS, 1, 1)).reshape(NKV * GROUPS, P).T
    par = np.concatenate([channels(a["conv_w"][0]), channels(a["conv_b"]), channels(a["conv_ln_g"]),
                          channels(a["conv_ln_b"]), ftaps, fbias, sinks], axis=1)
    assert par.shape == (P, PAR_N)
    w_o = a["w_o"][0]
    heads = w_o[:DC].reshape(2, NQ // 2, HEAD, D).transpose(1, 0, 2, 3).reshape(NQ // 2, P, D)
    con = np.zeros((P, CON_N), np.float32)
    con[:, CON_ID:CON_ID + P] = np.eye(P)
    for base in (0, HEAD):
        for i in range(ROT // 2):
            con[base + ROT // 2 + i, CON_ROT + base + i] = -1.0
            con[base + i, CON_ROT + base + ROT // 2 + i] = 1.0
            con[[base + i, base + ROT // 2 + i], CON_FREQ] = ROPE_THETA ** (-i / (ROT // 2))
    con[:, CON_ONES:CON_ONES + P] = 1 / DC
    return {
        "x": a["x"][0], "positions": a["positions"], "in_ln_g": a["in_ln_g"], "in_ln_b": a["in_ln_b"],
        "w_in": columns(a["w_in"][0], IN_TILES), "w_o": np.ascontiguousarray(
            np.concatenate([heads, w_o[DC:].reshape(CT, P, D)]).transpose(1, 0, 2)),
        "w_up": columns(a["w_up"][0], ffn_order), "w_down": a["w_down"][0].reshape(FT, P, D),
        "ln1_g": a["ln1_g"][0], "ln1_b": a["ln1_b"][0], "ln2_g": a["ln2_g"][0], "ln2_b": a["ln2_b"][0],
        "par": np.ascontiguousarray(par), "con": con,
    }


def kernel(**inputs):
    import concourse.bacc as bacc
    from concourse.bass_utils import run_bass_kernel_spmd

    arrays = lay_out(inputs)
    nc = bacc.Bacc("TRN2", target_bir_lowering=False, num_devices=1)
    io = {k: nc.dram_tensor(k, v.shape, mybir.dt.from_np(v.dtype), kind="ExternalInput").ap() for k, v in arrays.items()}
    out = nc.dram_tensor("out", (1, SEQ, D), F32, kind="ExternalOutput").ap()
    build(nc, io, out)
    r = run_bass_kernel_spmd(nc, [arrays], core_ids=[0])
    return r.results[0]["out"]
```

```python
from contextlib import ExitStack

import numpy as np
import concourse.bass as bass
from concourse import mybir

F32 = mybir.dt.float32
F32R = mybir.dt.float32r
I32 = mybir.dt.int32
ALU = mybir.AluOpType
ACT = mybir.ActivationFunctionType
AX = mybir.AxisListType

P = 128
SEQ = 2048
D = 1024
HEAD = 64
CHUNK = 64
NQ, NKV = 8, 2
QKV = (NQ + 2 * NKV) * HEAD
DC = 512
TAPS = 31
HALO = TAPS - 1
ACT_TAPS = 9
DFF = 2816
FTAPS = 3
EPS = 1e-5
ROT = HEAD // 4
ROPE_THETA = 500000.0
ALPHA = 2.0 ** 0.25
KT = D // P
NT = SEQ // P
BLK = 512
NB = SEQ // BLK
RB = BLK // P
CT = DC // P
QT = QKV // P
FT = DFF // P
HALF = FT // 2

STREAM = [("a", 0), ("gate", 0)]
for _j in range(1, CT):
    STREAM += [("a", _j), ("gate", _j), ("qkv", _j - 1)]
STREAM += [("qkv", _j) for _j in range(CT - 1, QT)]
IN_TILES = [{"a": QT, "gate": QT + CT, "qkv": 0}[_kind] + _j for _kind, _j in STREAM]

PAR_TAPS = 0
PAR_CB = PAR_TAPS + CT * TAPS
PAR_LNG = PAR_CB + CT
PAR_LNB = PAR_LNG + CT
PAR_FTAPS = PAR_LNB + CT
PAR_FB = PAR_FTAPS + 2 * FT * FTAPS
PAR_SINK = PAR_FB + 2 * FT
PAR_N = PAR_SINK + NKV * 4
CON_ID, CON_ROT, CON_ONES, CON_FREQ = 0, P, 2 * P, 3 * P
CON_N = 3 * P + 4

TWO_PI = 2 * np.pi
PI_1 = 6.28125
PI_2 = float(np.float32(round((TWO_PI - PI_1) * 2 ** 17) / 2 ** 17))
PI_3 = float(np.float32(TWO_PI - PI_1 - PI_2))
ROUND = 1.5 * 2.0 ** 23
BELOW_PI = 3.1415925


class Count:

    def __init__(self, sem, eng):
        self.sem, self.eng, self.base, self.n = sem, eng, 0, 0

    def inc(self, ins):
        ins.then_inc(self.sem, 1)
        self.n += 1
        return self.n

    def wait(self, n=None):
        self.eng.wait_ge(self.sem, self.base + (self.n if n is None else n))


def row_to_all(ap):
    return ap.rearrange("(o n) -> o n", o=1).broadcast_to([P, ap.shape[0]])


def refine_rstd(nc, chain, rstd, v, y, t):
    chain.wait()
    chain.inc(nc.vector.tensor_tensor(t, y, y, ALU.mult))
    chain.wait()
    chain.inc(nc.vector.scalar_tensor_tensor(out=t, in0=t, scalar=-0.5, in1=v, op0=ALU.mult, op1=ALU.mult))
    chain.wait()
    chain.inc(nc.vector.scalar_tensor_tensor(out=rstd, in0=t, scalar=1.5, in1=y, op0=ALU.add, op1=ALU.mult))


def phase_project(nc, x, positions, ln_g, ln_b, w_tiles, par, con, h_scr, qkv_scr, conv_scr, trig_scr):
    ctx = ExitStack()
    with ctx:
        def sb(name, shape, dt=F32):
            return ctx.enter_context(nc.sbuf_tensor(name, shape, dt))

        def sem(name):
            return ctx.enter_context(nc.semaphore(name))

        hT_hi = sb("a_hT_hi", [P, KT, SEQ], F32R)
        hT_lo = sb("a_hT_lo", [P, KT, SEQ], F32R)
        w_raw = sb("a_w_raw", [P, 2, KT, P])
        w_hi = sb("a_w_hi", [P, 2, KT, P], F32R)
        w_lo = sb("a_w_lo", [P, 2, KT, P], F32R)
        glu = sb("a_glu", [P, 2, HALO + SEQ])
        sig = sb("a_sig", [P, BLK])
        q_out = sb("a_q_out", [P, 2, BLK])
        spare = sb("a_spare", [P, D])
        xs = sb("a_xs", [P, RB, D])
        hs = [glu[:, 1, 0:D], glu[:, 1, D:2 * D], q_out[:, :, :].rearrange("p s t -> p (s t)"), spare[:]]
        prod = spare[:].rearrange("p (s t) -> p s t", s=2)
        conv_out = xs[:, :, :].rearrange("p (s a) d -> p s (a d)", s=2)
        gb = sb("a_gb", [P, 2, D])
        g_bc, b_bc = gb[:, 0, :], gb[:, 1, :]
        part = gb[:, :, :].rearrange("p s t -> p (s t)")
        ident = sb("a_ident", [P, P])
        taps = sb("a_taps", [P, CT, TAPS])
        cbias = sb("a_cbias", [P, CT])
        stat = sb("a_stat", [P, RB, 2, 6])
        mv = sb("a_mv", [P, RB, 2])
        vs = sb("a_vs", [P, 5, RB])
        veps, root, inv, tmp, rstd = (vs[:, k, :] for k in range(5))
        nmr = sb("a_nmr", [P, RB])
        ang, turns, freq = sb("a_ang", [P, P]), sb("a_turns", [P, P]), sb("a_freq", [P, 4])
        trig = sb("a_trig", [P, 2, P])
        pos = sb("a_pos", [P, P], I32)
        half_pi = sb("a_half_pi", [P, 1])
        mm = [ctx.enter_context(nc.psum_tensor(f"a_mm{k}", [P, BLK], F32)) for k in range(4)]
        acc = ctx.enter_context(nc.psum_tensor("a_acc", [P, SEQ], F32))
        tp = [acc[:, k * D:(k + 1) * D].rearrange("p (k t) -> p k t", k=KT) for k in range(2)]

        con_ld, par_ld = sem("a_con_ld"), sem("a_par_ld")
        x_ld = [sem(f"a_x_ld{r}") for r in range(RB)]
        h_st = [sem(f"a_h_st{r}") for r in range(RB)]
        w_ld = [sem(f"a_w_ld{s}") for s in range(2)]
        veps_ok, root_ok, nmr_ok = sem("a_veps"), sem("a_root"), sem("a_nmr")
        norm_ok, scaled_ok, h_ok = sem("a_norm"), sem("a_scaled"), sem("a_h")
        tp_ok, tp_free, hi_ok, lo_ok = sem("a_tp"), sem("a_tp_free"), sem("a_hi"), sem("a_lo")
        whi_ok, wlo_ok = sem("a_whi"), sem("a_wlo")
        mm_ok, mm_free = sem("a_mm"), sem("a_mm_free")
        pad_ok, glu_ok = sem("a_pad"), sem("a_glu")
        conv_ok, conv_free, dve_seq = sem("a_conv"), sem("a_conv_free"), sem("a_dve")
        stats_seen, prod_ok, part_ok = sem("a_stats_seen"), sem("a_prod"), sem("a_part")
        q_st = [sem(f"a_q_st{s}") for s in range(2)]
        c_st = [sem(f"a_c_st{s}") for s in range(2)]
        pos_ld, ang_seq, ang_ok, trig_ok, trig_st = (sem("a_" + n) for n in ("pos_ld", "ang_seq", "ang", "trig", "trig_st"))
        half_pi_ok = sem("a_half_pi_ok")
        block = ctx.enter_context(nc.Block())

        def tap_of(j, k):
            return taps[:, bass.ds(j, 1), k:k + 1].rearrange("p o t -> p (o t)")

        @block.sync
        def _(sp):
            sp.dma_start(ident[:], con[:, CON_ID:CON_ID + P]).then_inc(con_ld, 16)
            for r in range(RB):
                sp.dma_start(xs[:, r, :], x[bass.ts(r, P), :]).then_inc(x_ld[r], 16)
            sp.dma_start(g_bc, row_to_all(ln_g)).then_inc(par_ld, 16)
            sp.dma_start(b_bc, row_to_all(ln_b)).then_inc(par_ld, 16)
            sp.dma_start(taps[:], par[:, PAR_TAPS:PAR_TAPS + CT * TAPS].rearrange("p (c t) -> p c t", c=CT)).then_inc(par_ld, 16)
            sp.dma_start(cbias[:], par[:, PAR_CB:PAR_CB + CT]).then_inc(par_ld, 16)
            for s in range(2):
                sp.dma_start(w_raw[:, s, :, :], w_tiles[s, :, :, :]).then_inc(w_ld[s], 16)

            def reload(n, r):
                sp.wait_ge(norm_ok, RB * n + (r + 1))
                sp.dma_start(xs[:, r, :], x[bass.ds((n * RB + (RB + r)) * P, P), :]).then_inc(x_ld[r], 16)

            def store(n, r):
                sp.wait_ge(h_ok, RB * n + (r + 1))
                sp.dma_start(h_scr[bass.ds(RB * n + r, 1), :, :].rearrange("o p d -> p (o d)"), hs[r]).then_inc(h_st[r], 16)

            with sp.Fori(0, NB - 1) as n:
                reload(n, 0)
                for r in range(1, RB):
                    reload(n, r)
                    store(n, r - 1)
                store(n, RB - 1)
            for r in range(RB):
                store(NB - 1, r)
            with sp.Fori(0, CT - 1) as j:
                for u in range(4):
                    sp.wait_ge(wlo_ok, 4 * j + (u + 1))
                    sp.dma_start(w_raw[:, u % 2, :, :], w_tiles[bass.ds(4 * j + (u + 2), 1), :, :, :].rearrange("o p k c -> p (o k) c")).then_inc(w_ld[u % 2], 16)
            for r in range(RB):
                sp.wait_ge(h_st[r], 16 * NB)

        @block.scalar
        def _(act):
            def weights_hi(nth, slot):
                act.wait_ge(w_ld[slot], nth * 16)
                nc.scalar.copy(w_hi[:, slot, :, :], w_raw[:, slot, :, :]).then_inc(whi_ok, 1)

            def block_root(n):
                act.wait_ge(veps_ok, n + 1)
                nc.scalar.activation(root, veps, ACT.Sqrt).then_inc(root_ok, 1)

            def norm(n, r):
                act.wait_ge(nmr_ok, n + 1)
                if not (isinstance(n, int) and n == 0):
                    act.wait_ge(h_st[r], n * 16)
                nc.scalar.activation(hs[r], xs[:, r, :], ACT.Identity, bias=nmr[:, r:r + 1],
                                     scale=rstd[:, r:r + 1]).then_inc(norm_ok, 1)

            def hi_of(n, r):
                act.wait_ge(tp_ok, RB * n + (r + 1))
                nc.scalar.copy(hT_hi[:, :, bass.ds((RB * n + r) * P, P)], tp[r % 2]).then_inc(hi_ok, 1)

            def take_a(e, slot, col, bank):
                act.wait_ge(mm_ok, e + 1)
                nc.scalar.copy(glu[:, slot, bass.ds(col, BLK)], mm[bank][:]).then_inc(mm_free, 1)

            def take_gate(e, k, bank):
                act.wait_ge(mm_ok, e + 1)
                act.wait_ge(glu_ok, k + 1)
                nc.scalar.activation(sig[:], mm[bank][:], ACT.Sigmoid).then_inc(mm_free, 1)

            nc.scalar.preload_act_table(ACT.Sqrt)
            act.sem_inc(mm_free, 2)
            act.sem_inc(conv_ok, 1)
            act.sem_inc(q_st[0], 16)
            act.sem_inc(q_st[1], 16)
            block_root(0)
            for r in range(RB):
                norm(0, r)
            weights_hi(1, 0)
            weights_hi(1, 1)

            def block(n, first, last):
                hi_of(n, 0)
                hi_of(n, 1)
                if not first:
                    take_a(2 * n - 2, 0, n * BLK + (HALO - BLK), 2)
                if not last:
                    block_root(n + 1)
                hi_of(n, 2)
                if not last:
                    norm(n + 1, 0)
                hi_of(n, 3)
                if not last:
                    for r in range(1, RB):
                        norm(n + 1, r)
                if not first:
                    take_gate(2 * n - 1, n - 1, 3)

            block(0, True, False)
            for f in range(ROT // 2):
                act.dma_start(pos[f * NT:(f + 1) * NT, :], positions.rearrange("o (t q) -> (o t) q", t=NT)).then_inc(pos_ld, 16)
            act.dma_start(freq[:], con[:, CON_FREQ:CON_FREQ + 4]).then_inc(pos_ld, 16)
            with act.Fori(1, NB - 1) as n:
                block(n, False, False)
            block(NB - 1, False, True)
            take_a(2 * NB - 2, 0, (NB - 1) * BLK + HALO, 2)
            weights_hi(2, 0)
            take_gate(2 * NB - 1, NB - 1, 3)
            weights_hi(2, 1)
            act.wait_ge(half_pi_ok, 1)
            act.wait_ge(ang_ok, 2)
            nc.scalar.activation(trig[:, 0, :], turns[:], ACT.Sin, bias=half_pi[:], scale=-1.0).then_inc(trig_ok, 1)
            nc.scalar.activation(trig[:, 1, :], ang[:], ACT.Sin).then_inc(trig_ok, 1)
            act.wait_ge(trig_ok, 2)
            act.dma_start(trig_scr.rearrange("c f (t q) -> (f t) c q", t=NT), trig[:, :, :]).then_inc(trig_st, 16)
            for r in range(RB):
                act.wait_ge(h_st[r], 16 * NB)
            act.sem_inc(conv_free, 32)

            def tap_products(j, at):
                for i in range(at * ACT_TAPS // 2, (at + 1) * ACT_TAPS // 2):
                    k, c = divmod(i, NB)
                    if i == 0:
                        act.wait_ge(glu_ok, NB * j + (NB + 1))
                        act.wait_ge(conv_ok, j + 1)
                    if k:
                        act.wait_ge(part_ok, (ACT_TAPS - 1) * NB * j + (i - NB + 1))
                    dst = prod[:, i % 2, :] if k else part[:, c * BLK:(c + 1) * BLK]
                    nc.scalar.activation(dst, glu[:, j % 2, bass.ds(c * BLK + k, BLK)], ACT.Copy, scale=tap_of(j, k)).then_inc(prod_ok, 1)

            def store_q(e, k):
                act.wait_ge(mm_free, e + 3)
                act.dma_start(qkv_scr[k // NB, :, bass.ts(k % NB, BLK)], q_out[:, k % 2, :]).then_inc(q_st[k % 2], 16)

            def take_qkv(i, j):
                for n in range(NB):
                    e, k = NB * i + n, NB * j + n
                    act.wait_ge(mm_ok, e + 1)
                    act.wait_ge(q_st[k % 2], 16 * (k // 2 + 1))
                    nc.scalar.copy(q_out[:, k % 2, :], mm[n][:]).then_inc(mm_free, 1)
                    if n:
                        store_q(e - 1, k - 1)
                    if j >= CT - 1:
                        last_tap_products(NB * (j - CT + 1) + n)
                store_q(e, k)

            def store_conv(j):
                act.wait_ge(conv_ok, j + 2)
                act.wait_ge(conv_free, 16 * (j + 2))
                act.dma_start(conv_scr[j, :, :], conv_out[:, j % 2, :]).then_inc(conv_free, 16)

            def last_tap_products(at):
                if at < 2 * NB:
                    tap_products(CT - 1, at)

            for i, (kind, j) in enumerate(STREAM[2:], 2):
                for n in range(NB):
                    if kind == "a":
                        if n == 0:
                            act.wait_ge(conv_ok, j)
                        take_a(NB * i + n, j % 2, n * BLK + HALO, n)
                        tap_products(j - 1, n)
                    elif kind == "gate":
                        take_gate(NB * i + n, NB * j + n, n)
                        tap_products(j - 1, NB + n)
                if kind == "qkv":
                    take_qkv(i, j)
                if i + 2 < len(STREAM):
                    weights_hi(i // 2 + 2, i % 2)
                if kind == "qkv" and j < CT - 1:
                    store_conv(j)
            store_conv(CT - 1)
            act.wait_ge(conv_free, 16 * (CT + 2))
            for s in range(2):
                act.wait_ge(q_st[s], 16 * (QT * NB // 2 + 1))
            act.wait_ge(trig_st, 16)

        @block.gpsimd
        def _(pool):
            nc.gpsimd.memset(half_pi[:], float(np.pi / 2)).then_inc(half_pi_ok, 1)
            nc.gpsimd.memset(glu[:, 0, 0:HALO], 0.0).then_inc(glu_ok, 1)

            def weights_lo(s, slot):
                pool.wait_ge(whi_ok, s + 1)
                nc.gpsimd.tensor_tensor(w_lo[:, slot, :, :], w_raw[:, slot, :, :], w_hi[:, slot, :, :].bitcast(F32),
                                        ALU.subtract).then_inc(wlo_ok, 1)

            def add_bias(n, r):
                pool.wait_ge(scaled_ok, RB * n + (r + 1))
                nc.gpsimd.tensor_tensor(hs[r], hs[r], b_bc, ALU.add).then_inc(h_ok, 1)

            def gate(e, slot, col):
                pool.wait_ge(mm_free, e + 3)
                v = glu[:, slot, bass.ds(col, BLK)]
                nc.gpsimd.tensor_tensor(v, v, sig[:], ALU.mult).then_inc(glu_ok, 1)

            pool.sem_inc(part_ok, 2)
            pool.wait_ge(par_ld, 64)
            for r in range(RB):
                add_bias(0, r)
            weights_lo(0, 0)
            weights_lo(1, 1)
            add_bias(1, 0)
            add_bias(1, 1)
            with pool.Fori(1, NB - 1) as n:
                add_bias(n, 2)
                add_bias(n, 3)
                add_bias(n + 1, 0)
                add_bias(n + 1, 1)
                gate(2 * n - 1, 0, n * BLK + (HALO - BLK))
            add_bias(NB - 1, 2)
            add_bias(NB - 1, 3)
            gate(2 * NB - 3, 0, (NB - 2) * BLK + HALO)
            weights_lo(2, 0)
            gate(2 * NB - 1, 0, (NB - 1) * BLK + HALO)
            weights_lo(3, 1)
            pool.wait_ge(h_st[0], 16 * NB)
            pool.wait_ge(tp_ok, NT)
            nc.gpsimd.memset(glu[:, 1, 0:HALO], 0.0).then_inc(pad_ok, 1)

            def tap_sums(j, at):
                for i in range(at * ACT_TAPS // 2, (at + 1) * ACT_TAPS // 2):
                    k, c = divmod(i, NB)
                    if k == 0:
                        continue
                    pool.wait_ge(prod_ok, ACT_TAPS * NB * j + (i + 1))
                    if k > 1:
                        pool.wait_ge(part_ok, (ACT_TAPS - 1) * NB * j + (i - 2 * NB + 3))
                    p = part[:, c * BLK:(c + 1) * BLK]
                    nc.gpsimd.tensor_tensor(p, p, prod[:, i % 2, :], ALU.add).then_inc(part_ok, 1)

            for i, (kind, j) in enumerate(STREAM[2:], 2):
                for n in range(NB):
                    if kind == "a":
                        tap_sums(j - 1, n)
                    elif kind == "gate":
                        gate(NB * i + n, j % 2, n * BLK + HALO)
                        tap_sums(j - 1, NB + n)
                    elif 0 <= j - (CT - 1) < 2:
                        tap_sums(CT - 1, NB * (j - (CT - 1)) + n)
                if i + 2 < len(STREAM):
                    weights_lo(i + 2, i % 2)

        @block.vector
        def _(dve):
            chain = Count(dve_seq, dve)

            STEPS = 2 * RB + RB + 4

            def stats(n, r):
                chain.base, chain.n = n * STEPS, 2 * r
                dve.wait_ge(x_ld[r], n * 16 + 16)
                for a in range(2):
                    chain.inc(nc.vector.bn_stats(stat[:, r, a, :], xs[:, r, a * BLK:(a + 1) * BLK]))

            def block_stats(n):
                chain.wait()
                dve.sem_inc(stats_seen, 1)
                for r in range(RB):
                    chain.inc(nc.vector.bn_aggr(mv[:, r, :], stat[:, r, :, :].rearrange("p a s -> p (a s)")))
                chain.wait()
                nc.vector.tensor_scalar(veps, mv[:, :, 1], EPS, None, ALU.add).then_inc(veps_ok, 1)
                dve.wait_ge(root_ok, n + 1)
                chain.inc(nc.vector.reciprocal(inv, root))
                dve.wait_ge(veps_ok, n + 1)
                refine_rstd(nc, chain, rstd, veps, inv, tmp)
                chain.wait()
                nc.vector.scalar_tensor_tensor(out=nmr[:], in0=mv[:, :, 0], scalar=-1.0, in1=rstd, op0=ALU.mult,
                                               op1=ALU.mult).then_inc(nmr_ok, 1)
                assert chain.n == STEPS

            def scale(n, r):
                dve.wait_ge(norm_ok, RB * n + (r + 1))
                nc.vector.tensor_tensor(hs[r], hs[r], g_bc, ALU.mult).then_inc(scaled_ok, 1)

            def lo_of(n, r):
                dve.wait_ge(hi_ok, RB * n + (r + 1))
                at = bass.ds((RB * n + r) * P, P)
                nc.vector.tensor_tensor(hT_lo[:, :, at], tp[r % 2], hT_hi[:, :, at].bitcast(F32), ALU.subtract).then_inc(lo_ok, 1)

            def block(n, last):
                scale(n, 2)
                scale(n, 3)
                lo_of(n, 0)
                if last:
                    for r in range(1, RB):
                        lo_of(n, r)
                    return
                stats(n + 1, 0)
                stats(n + 1, 1)
                lo_of(n, 1)
                stats(n + 1, 2)
                stats(n + 1, 3)
                block_stats(n + 1)
                lo_of(n, 2)
                scale(n + 1, 0)
                lo_of(n, 3)
                scale(n + 1, 1)

            for r in range(RB):
                stats(0, r)
            block_stats(0)
            dve.wait_ge(par_ld, 64)
            scale(0, 0)
            scale(0, 1)
            with dve.Fori(0, NB - 1) as n:
                block(n, False)
            block(NB - 1, True)

            seq = Count(ang_seq, dve)
            dve.wait_ge(pos_ld, 16 * (ROT // 2 + 1))
            seq.inc(nc.vector.tensor_copy(ang[:], pos[:]))
            seq.wait()
            seq.inc(nc.vector.tensor_scalar(ang[:], ang[:], freq[:, 0:1], None, ALU.mult))
            seq.wait()
            seq.inc(nc.vector.tensor_scalar(turns[:], ang[:], 1 / TWO_PI, ROUND, ALU.mult, ALU.add))
            seq.wait()
            seq.inc(nc.vector.tensor_scalar(turns[:], turns[:], ROUND, None, ALU.subtract))
            for pi_k in (PI_1, PI_2, PI_3):
                seq.wait()
                seq.inc(nc.vector.scalar_tensor_tensor(out=ang[:], in0=turns[:], scalar=-pi_k, in1=ang[:], op0=ALU.mult, op1=ALU.add))
            seq.wait()
            nc.vector.tensor_scalar(ang[:], ang[:], BELOW_PI, -BELOW_PI, ALU.min, ALU.max).then_inc(ang_ok, 1)
            dve.wait_ge(ang_ok, 1)
            nc.vector.scalar_tensor_tensor(out=turns[:], in0=ang[:], scalar=-1.0, in1=ang[:], op0=ALU.mult, op1=ALU.max).then_inc(ang_ok, 1)

            dve.wait_ge(pad_ok, 1)
            with dve.Fori(0, CT) as j:
                dve.wait_ge(glu_ok, NB * j + (NB + 1))
                chain.base, chain.n = j * (TAPS - ACT_TAPS) + NB * STEPS, 0
                dve.wait_ge(conv_ok, j + 1)
                for k in range(ACT_TAPS, TAPS):
                    src = glu[:, bass.ds(j % 2, 1), k:k + SEQ].rearrange("p o t -> p (o t)")
                    if k == ACT_TAPS:
                        v = nc.vector.tensor_scalar(acc[:], src, tap_of(j, k), cbias[:, bass.ds(j, 1)], ALU.mult, ALU.add)
                    else:
                        chain.wait()
                        v = nc.vector.scalar_tensor_tensor(out=acc[:], in0=src, scalar=tap_of(j, k), in1=acc[:],
                                                           op0=ALU.mult, op1=ALU.add)
                    chain.inc(v)
                chain.wait()
                dve.wait_ge(part_ok, (ACT_TAPS - 1) * NB * (j + 1) + 2)
                dve.wait_ge(conv_free, 16 * (j + 1))
                nc.vector.tensor_tensor(conv_out[:, bass.ds(j % 2, 1), :].rearrange("p o t -> p (o t)"), acc[:], part,
                                        ALU.add).then_inc(conv_ok, 1)

        @block.tensor
        def _(pe):
            def transposes(n, r):
                pe.wait_ge(h_ok, RB * n + (r + 1))
                for k in range(KT):
                    last = nc.tensor.transpose(tp[r % 2][:, k, :], hs[r][:, bass.ts(k, P)], ident[:])
                last.then_inc(tp_ok, 1)

            def products(slot, ks, rhs_at, bank, done):
                for k in ks:
                    for w, h in ((w_hi, hT_hi), (w_hi, hT_lo), (w_lo, hT_hi)):
                        last = nc.tensor.matmul(mm[bank][:], w[:, slot, k, :], h[:, k, rhs_at],
                                                start=(k == 0 and w is w_hi and h is hT_hi),
                                                stop=(k == KT - 1 and w is w_lo))
                if done:
                    last.then_inc(mm_ok, 1)

            def sweep(n, m, half):
                if half == 0:
                    pe.wait_ge(mm_free, 2 * n + (m + 1))
                products(m, range(half * KT // 2, (half + 1) * KT // 2), bass.ds(n * BLK, BLK), 2 + m, half == 1)

            pe.wait_ge(con_ld, 16)
            for r in range(RB):
                if r >= 2:
                    pe.wait_ge(lo_ok, r - 1)
                transposes(0, r)
            pe.wait_ge(wlo_ok, 2)
            with pe.Fori(1, NB) as n:
                pe.wait_ge(lo_ok, RB * n)
                for r in range(RB):
                    pe.wait_ge(lo_ok, RB * n + (r - 1))
                    transposes(n, r)
                    sweep(n - 1, r // 2, r % 2)
            pe.wait_ge(lo_ok, NT)
            for m in range(2):
                for half in range(2):
                    sweep(NB - 1, m, half)

            with pe.Fori(0, CT - 1) as j:
                for u in range(4):
                    pe.wait_ge(wlo_ok, 4 * j + (u + 3))
                    for n in range(NB):
                        pe.wait_ge(mm_free, 4 * NB * j + (2 * NB + NB * u + n - 1))
                        products(u % 2, range(KT), bass.ts(n, BLK), n, True)


class Tile:

    def __init__(self, i, k):
        self.t, self.slot, self.nth = 2 * i + k, k % 2, i + k // 2

    def tokens(self):
        return bass.ts(self.t, P) if isinstance(self.t, int) else bass.ds(self.t * P, P)


def after(eng, sem, value):
    if not isinstance(value, int) or value > 0:
        eng.wait_ge(sem, value)


def each(ap, n):
    return ap.unsqueeze(1).broadcast_to([P, n, ap.shape[1]])


def along(ap, n):
    return ap.unsqueeze(2).broadcast_to([P, ap.shape[1], n])


MASKED = -3.0e38
SCALE = HEAD ** -0.5
CHUNKS = P // CHUNK
GROUPS = 4
KEYS = 2 * CHUNK
WO_SLOTS = 6
WO_POOL = (4, 5)


def phase_mix(nc, trig_scr, par, con, w_o, ln_g, ln_b, h_scr, qkv_scr, conv_scr, h1_scr, h1T_scr):
    ctx = ExitStack()
    with ctx:
        def sb(name, shape, dt=F32):
            return ctx.enter_context(nc.sbuf_tensor(name, shape, dt))

        def ps(name, shape):
            return ctx.enter_context(nc.psum_tensor(name, shape, F32))

        def sem(name):
            return ctx.enter_context(nc.semaphore(name))

        wo_hi = sb("m_wo_hi", [P, KT, D], F32R)
        wo_lo = sb("m_wo_lo", [P, KT, D], F32R)
        mix_hi = sb("m_mix_hi", [P, 2, KT, P], F32R)
        mix_lo = sb("m_mix_lo", [P, 2, KT, P], F32R)
        ident, rot, ones = sb("m_ident", [P, P]), sb("m_rot", [P, P]), sb("m_ones", [P, P])
        eps, one = sb("m_eps", [P, 1]), sb("m_one", [P, 1])
        cg, cb, sink = sb("m_cg", [P, CT]), sb("m_cb", [P, CT]), sb("m_sink", [P, NKV, GROUPS])
        g_bc, b_bc = sb("m_g", [P, D]), sb("m_b", [P, D])
        cos, sin = sb("m_cos", [P, SEQ]), sb("m_sin", [P, SEQ])
        wo_raw = sb("m_wo_raw", [P, WO_SLOTS, D])
        qk_in = sb("m_qk_in", [P, 2, 5, P])
        v_in = sb("m_v_in", [P, 2, CHUNK + P])
        conv_in = sb("m_conv_in", [P, 2, CT, P])
        h_in = sb("m_h_in", [P, 2, D])
        qk_cos, qk_sin = sb("m_qk_cos", [P, 5, P]), sb("m_qk_sin", [P, 5, P])
        qr, kr = sb("m_qr", [P, CHUNKS, 4 * CHUNK]), sb("m_kr", [P, CHUNK + P])
        vw = sb("m_vw", [P, CHUNKS, P])
        prob = sb("m_prob", [P, NKV, GROUPS, KEYS + 1])
        top, peak = sb("m_top", [P, NKV, GROUPS]), sb("m_peak", [P, NKV, GROUPS])
        den, inv = sb("m_den", [P, NKV, GROUPS]), sb("m_inv", [P, NKV, GROUPS])
        probT = sb("m_probT", [P, NKV, BLK])
        cc, cz, ce = sb("m_cc", [P, CT, P]), sb("m_cz", [P, CT, P]), sb("m_ce", [P, CT, P])
        squares, sw = sb("m_squares", [P, CT, P]), sb("m_sw", [P, CT, P])
        cv, cy, ct, cr, cln = (sb(f"m_c{k}", [P, P]) for k in range(5))
        r = sb("m_r", [P, 2, D])
        h1T = sb("m_h1T", [P, 2, KT, P])
        stat, mv = sb("m_stat", [P, 2, 6]), sb("m_mv", [P, 2])
        lv, ly, lt, lr = (sb(f"m_l{k}", [P, 1]) for k in range(4))

        y = ps("m_y", [P, D])
        rq = ps("m_rq", [P, 4, P])
        aux = ps("m_aux", [P, BLK])
        score = [ps(f"m_score{g}", [P, GROUPS, KEYS]) for g in range(NKV)]
        tps = ps("m_tps", [P, 2 * BLK])
        mean = var = aux[:, 0:P]
        rk = aux[:, P:2 * P]
        vT = tps[:, BLK:BLK + 2 * P].rearrange("p (c k) -> p c k", c=CHUNKS)
        pv = score[0][:, :, :].rearrange("p g k -> p (g k)").rearrange("p (c t q) -> p c t q", c=CHUNKS, t=4)

        con_ld, trig_ld, row_ld = sem("m_con_ld"), sem("m_trig_ld"), sem("m_row_ld")
        wo_ld = [sem(f"m_wo_ld{s}") for s in range(WO_SLOTS)]
        in_ld = [sem(f"m_in_ld{s}") for s in range(2)]
        h_ld = [sem(f"m_h_ld{s}") for s in range(2)]
        h1_st = [sem(f"m_h1_st{s}") for s in range(2)]
        h1T_st = [sem(f"m_h1T_st{s}") for s in range(2)]
        wo_hi_ok, wo_lo_ok, pads_ok = sem("m_wo_hi"), sem("m_wo_lo"), sem("m_pads")
        cos_pad, sin_pad, wo_lo_pool_ok = sem("m_cos_pad"), sem("m_sin_pad"), sem("m_wo_lo_pool")
        rq_ps, rk_ps, mean_ps, var_ps, vT_ps = (sem("m_" + n) for n in ("rq_ps", "rk_ps", "mean_ps", "var_ps", "vT_ps"))
        score_ps, probT_ps, pv_ps, y_ps, h1T_ps = (sem("m_" + n) for n in ("score_ps", "probT_ps", "pv_ps", "y_ps", "h1T_ps"))
        cos_ok, kcopy_ok, sin_qk_ok, qr_ok, kr_ok = (sem("m_" + n) for n in ("cos", "kcopy", "sin_qk", "qr", "kr"))
        centre_ok, square_ok, cy_ok, cn_ok, gate_ok, gate_exp_ok, swish_ok = (sem("m_" + n) for n in ("centre", "square", "cy", "cn", "gate", "gate_exp", "swish"))
        conv_hi_ok, conv_lo_ok, attn_hi_ok, attn_lo_ok = (sem("m_" + n) for n in ("conv_hi", "conv_lo", "attn_hi", "attn_lo"))
        vw_ok, shift_ok, exp_ok, prob_ok, probT_ok = (sem("m_" + n) for n in ("vw", "shift", "exp", "prob", "probT"))
        resid_ok, lv_ok, ly_ok, norm_ok, scaled_ok, h1_ok, h1T_ok = (sem("m_" + n) for n in ("resid", "lv", "ly", "norm", "scaled", "h1", "h1T"))
        soft_seq, cn_seq, ln_seq, z_seq, lact_seq, cact_seq, stats_seen = (sem("m_" + n) for n in ("soft_seq", "cn_seq", "ln_seq", "z_seq", "lact_seq", "cact_seq", "stats_seen"))
        block = ctx.enter_context(nc.Block())

        q_rows = qkv_scr.rearrange("q p t -> (q p) t")

        def steps(eng, first, step, last, final):
            first(Tile(0, 0))
            step(None, Tile(0, 0), Tile(0, 1))
            with eng.Fori(0, NT // 2 - 1) as i:
                step(Tile(i, 0), Tile(i, 1), Tile(i, 2))
                step(Tile(i, 1), Tile(i, 2), Tile(i, 3))
            last(Tile(NT // 2 - 1, 0), Tile(NT // 2 - 1, 1))
            final(Tile(NT // 2 - 1, 1))

        @block.sync
        def _(sp):
            def load_in(x):
                if isinstance(x.t, int) and x.t == 0:
                    v, at, n = v_in[:, 0, CHUNK:], 0, P
                else:
                    v, at, n = v_in[:, x.slot, :], x.t * P - CHUNK, P + CHUNK
                for g in range(NKV):
                    src = q_rows[4 * HEAD * g:4 * HEAD * (g + 1), x.tokens()].rearrange("(h d) t -> d h t", d=HEAD)
                    sp.dma_start(qk_in[HEAD * g:HEAD * (g + 1), x.slot, 0:4, :], src).then_inc(in_ld[x.slot], 16)
                sp.dma_start(qk_in[:, x.slot, 4, :], qkv_scr[4, :, x.tokens()]).then_inc(in_ld[x.slot], 16)
                sp.dma_start(v, qkv_scr[5, :, bass.ds(at, n)]).then_inc(in_ld[x.slot], 16)
                sp.dma_start(conv_in[:, x.slot, :, :], conv_scr[:, :, x.tokens()].rearrange("c p t -> p c t")).then_inc(in_ld[x.slot], 16)

            def load_h(x):
                sp.dma_start(h_in[:, x.slot, :], h_scr[bass.ds(x.t, 1), :, :].rearrange("o p d -> p (o d)")).then_inc(h_ld[x.slot], 16)

            def next_in(c, m):
                after(sp, qr_ok, c.t + 1)
                after(sp, kr_ok, c.t + 1)
                after(sp, vT_ps, c.t + 1)
                after(sp, centre_ok, c.t + 1)
                load_in(m)

            def load_wo(k):
                if k >= WO_SLOTS:
                    sp.wait_ge(wo_lo_ok, k - WO_SLOTS + 1)
                sp.dma_start(wo_raw[:, k % WO_SLOTS, :], w_o[:, k, :]).then_inc(wo_ld[k % WO_SLOTS], 16)

            load_in(Tile(0, 0))
            for dst, at, n in ((ident, CON_ID, P), (rot, CON_ROT, P), (ones, CON_ONES, P)):
                sp.dma_start(dst[:], con[:, at:at + n]).then_inc(con_ld, 16)
            for dst, at in ((cg[:], PAR_LNG), (cb[:], PAR_LNB)):
                sp.dma_start(dst, par[:, at:at + CT]).then_inc(con_ld, 16)
            sp.dma_start(sink[:, :, :], par[:, PAR_SINK:PAR_N].rearrange("p (g a) -> p g a", g=NKV)).then_inc(con_ld, 16)
            for dst, src, pad in ((cos, trig_scr[0], cos_pad), (sin, trig_scr[1], sin_pad)):
                sp.wait_ge(pad, 1)
                for at in (0, ROT // 2, HEAD, HEAD + ROT // 2):
                    sp.dma_start(dst[at:at + ROT // 2, :], src).then_inc(trig_ld, 16)
            load_wo(0)
            load_wo(1)
            load_in(Tile(0, 1))
            for k in range(2, WO_SLOTS):
                load_wo(k)
            load_h(Tile(0, 0))
            sp.dma_start(g_bc[:], row_to_all(ln_g)).then_inc(row_ld, 16)
            sp.dma_start(b_bc[:], row_to_all(ln_b)).then_inc(row_ld, 16)
            for k in range(WO_SLOTS, KT):
                load_wo(k)

            def step(p, c, n):
                if p is not None:
                    next_in(p, n)
                    sp.wait_ge(resid_ok, p.t + 1)
                load_h(n)

            steps(sp, lambda n: None, step, lambda p, c: None, lambda p: None)

        @block.gpsimd
        def _(pool):
            nc.gpsimd.memset(kr[:, P:P + CHUNK], 0.0).then_inc(pads_ok, 1)
            nc.gpsimd.memset(v_in[:, 0, 0:CHUNK], 0.0).then_inc(pads_ok, 1)
            nc.gpsimd.memset(eps[:], EPS).then_inc(pads_ok, 1)
            nc.gpsimd.memset(one[:], 1.0).then_inc(pads_ok, 1)
            nc.gpsimd.memset(sin[:], 0.0).then_inc(sin_pad, 1)

            for s in range(2):
                pool.sem_inc(h1_st[s], 16)
                pool.sem_inc(h1T_st[s], 16)

            def rotate(n):
                pool.wait_ge(in_ld[n.slot], n.nth * 80 + 80)
                after(pool, score_ps, NKV * n.t)
                tok = n.tokens()
                nc.gpsimd.tensor_tensor(qk_cos[:, :, :], qk_in[:, n.slot, :, :], each(cos[:, tok], 5), ALU.mult).then_inc(cos_ok, 1)
                nc.gpsimd.tensor_copy(kr[:, 0:CHUNK], kr[:, P:P + CHUNK]).then_inc(kcopy_ok, 1)
                pool.wait_ge(cos_ok, n.t + 1)
                pool.wait_ge(kcopy_ok, n.t + 1)
                pool.wait_ge(sin_qk_ok, 2 * n.t + 1)
                nc.gpsimd.tensor_tensor(kr[:, CHUNK:], qk_cos[:, 4, :], qk_sin[:, 4, :], ALU.add).then_inc(kr_ok, 1)
                pool.wait_ge(sin_qk_ok, 2 * n.t + 2)
                view = "p t (c q) -> p c t q"
                nc.gpsimd.tensor_tensor(qr[:, :, :].rearrange("p c (t q) -> p c t q", t=4),
                                        qk_cos[:, 0:4, :].rearrange(view, c=CHUNKS),
                                        qk_sin[:, 0:4, :].rearrange(view, c=CHUNKS), ALU.add).then_inc(qr_ok, 1)

            def affine(p):
                pool.wait_ge(norm_ok, p.t + 1)
                nc.gpsimd.tensor_tensor(r[:, p.slot, :], r[:, p.slot, :], g_bc[:], ALU.mult).then_inc(scaled_ok, 1)
                pool.wait_ge(scaled_ok, p.t + 1)
                nc.gpsimd.tensor_tensor(r[:, p.slot, :], r[:, p.slot, :], b_bc[:], ALU.add).then_inc(h1_ok, 1)

            def step(p, c, n):
                rotate(n)
                if p is not None:
                    affine(p)

            pool.wait_ge(trig_ld, 16 * 8)
            pool.wait_ge(pads_ok, 4)

            def first(n):
                rotate(n)
                for k in WO_POOL:
                    pool.wait_ge(wo_hi_ok, k + 1)
                    nc.gpsimd.tensor_tensor(wo_lo[:, k, :], wo_raw[:, k % WO_SLOTS, :], wo_hi[:, k, :].bitcast(F32),
                                            ALU.subtract).then_inc(wo_lo_pool_ok, 1)
                pool.wait_ge(row_ld, 32)

            steps(pool, first, step, lambda p, c: affine(p), affine)

        @block.scalar
        def _(act):
            act.sem_inc(h1T_ok, 1)
            act.wait_ge(pads_ok, 4)
            nc.scalar.preload_act_table_set("natural_log_exp_and_others")

            def wo_hi_of(ks):
                for k in ks:
                    act.wait_ge(wo_ld[k % WO_SLOTS], 16 * (k // WO_SLOTS + 1))
                    nc.scalar.copy(wo_hi[:, k, :], wo_raw[:, k % WO_SLOTS, :]).then_inc(wo_hi_ok, 1)

            def attn_hi(c):
                act.wait_ge(pv_ps, c.t + 1)
                nc.scalar.copy(mix_hi[:, c.slot, 0:4, :].rearrange("p t (c q) -> p c t q", c=CHUNKS), pv).then_inc(attn_hi_ok, 1)

            def square(n):
                act.wait_ge(centre_ok, n.t + 1)
                nc.scalar.activation(squares[:, :, :], cc[:, :, :], ACT.Square).then_inc(square_ok, 1)

            def exps(n, g):
                act.wait_ge(shift_ok, NKV * n.t + (g + 1))
                nc.scalar.activation(prob[:, g, :, :], prob[:, g, :, :], ACT.Exp).then_inc(exp_ok, 1)

            def conv_root(n):
                act.wait_ge(var_ps, n.t + 1)
                nc.scalar.activation(cln[:], var, ACT.Ln, bias=eps[:]).then_inc(cact_seq, 1)
                act.wait_ge(cact_seq, 4 * n.t + 1)
                nc.scalar.activation(cy[:], cln[:], ACT.Exp, scale=-0.5).then_inc(cy_ok, 1)

            def gates(n):
                act.wait_ge(cn_ok, n.t + 1)
                for j in range(CT):
                    last = nc.scalar.activation(cz[:, j, :], cc[:, j, :], ACT.Identity, bias=cb[:, j:j + 1], scale=cg[:, j:j + 1])
                last.then_inc(cact_seq, 1)
                act.wait_ge(cact_seq, 4 * n.t + 2)
                for step, (func, bias, scale) in enumerate(((ACT.Abs, None, 1.0), (ACT.Exp, None, -1.0), (ACT.Ln, one, 1.0))):
                    src = ce if step else cz
                    more = {} if bias is None else {"bias": bias[:]}
                    v = nc.scalar.activation(ce[:, :, :], src[:, :, :], func, scale=scale, **more)
                    v.then_inc(gate_ok if step == 2 else cact_seq, 1)
                    if step < 2:
                        act.wait_ge(cact_seq, 4 * n.t + (3 + step))

            def gates_exp(n):
                act.wait_ge(z_seq, n.t + 1)
                nc.scalar.activation(ce[:, :, :], ce[:, :, :], ACT.Exp).then_inc(gate_exp_ok, 1)

            def conv_hi(n):
                act.wait_ge(swish_ok, n.t + 1)
                nc.scalar.copy(mix_hi[:, n.slot, 4:8, :], sw[:, :, :]).then_inc(conv_hi_ok, 1)

            def row_root(p):
                act.wait_ge(lv_ok, p.t + 1)
                nc.scalar.activation(lt[:], lv[:], ACT.Ln).then_inc(lact_seq, 1)
                act.wait_ge(lact_seq, p.t + 1)
                nc.scalar.activation(ly[:], lt[:], ACT.Exp, scale=-0.5).then_inc(ly_ok, 1)

            def out_T(p):
                act.wait_ge(h1T_ps, p.t + 1)
                act.wait_ge(h1T_st[p.slot], 16 * p.nth + 16)
                nc.scalar.copy(h1T[:, p.slot, :, :], tps[:].rearrange("p (k t) -> p k t", k=KT)).then_inc(h1T_ok, 1)

            def store(p):
                act.wait_ge(h1_ok, p.t + 1)
                act.dma_start(h1_scr[bass.ds(p.t, 1), :, :].rearrange("o p d -> p (o d)"), r[:, p.slot, :]).then_inc(h1_st[p.slot], 16)
                act.wait_ge(h1T_ok, p.t + 2)
                act.dma_start(h1T_scr[:, :, p.tokens()].rearrange("k p t -> p k t"), h1T[:, p.slot, :, :]).then_inc(h1T_st[p.slot], 16)

            def probs_T(n):
                for g in range(NKV):
                    act.wait_ge(probT_ps, NKV * n.t + (g + 1))
                    nc.scalar.copy(probT[:, g, :], tps[:, g * BLK:(g + 1) * BLK]).then_inc(probT_ok, 1)

            def step(p, c, n):
                square(n)
                if c is None:
                    wo_hi_of(range(WO_POOL[-1] + 1))
                if p is not None:
                    row_root(p)
                if c is not None:
                    gates_exp(c)
                    conv_hi(c)
                exps(n, 0)
                conv_root(n)
                exps(n, 1)
                probs_T(n)
                attn_hi(n)
                gates(n)
                if p is not None:
                    out_T(p)
                    store(p)

            def last(p, c):
                gates_exp(c)
                conv_hi(c)
                row_root(p)
                out_T(p)
                store(p)

            def final(p):
                row_root(p)
                out_T(p)
                store(p)
                for s in range(2):
                    act.wait_ge(h1_st[s], 16 * (NT // 2 + 1))
                    act.wait_ge(h1T_st[s], 16 * (NT // 2 + 1))

            def first(n):
                step(None, None, n)
                wo_hi_of(range(WO_POOL[-1] + 1, KT))

            steps(act, first, step, last, final)

        @block.vector
        def _(dve):
            nc.vector.memset(cos[:], 1.0).then_inc(cos_pad, 1)
            dve.wait_ge(trig_ld, 16 * 8)
            dve.wait_ge(con_ld, 16 * 6)

            def wo_lo_of(ks):
                for k in ks:
                    dve.wait_ge(wo_hi_ok, k + 1)
                    nc.vector.tensor_tensor(wo_lo[:, k, :], wo_raw[:, k % WO_SLOTS, :], wo_hi[:, k, :].bitcast(F32),
                                            ALU.subtract).then_inc(wo_lo_ok, 1)

            def residual(p):
                dve.wait_ge(y_ps, p.t + 1)
                dve.wait_ge(h_ld[p.slot], 16 * p.nth + 16)
                dve.wait_ge(h1_st[p.slot], 16 * p.nth + 16)
                after(dve, h1T_ok, p.t)
                nc.vector.scalar_tensor_tensor(out=r[:, p.slot, :], in0=h_in[:, p.slot, :], scalar=ALPHA, in1=y[:],
                                               op0=ALU.mult, op1=ALU.add).then_inc(resid_ok, 1)

            def attn_lo(c):
                dve.wait_ge(attn_hi_ok, c.t + 1)
                view = "p t (c q) -> p c t q"
                nc.vector.tensor_tensor(mix_lo[:, c.slot, 0:4, :].rearrange(view, c=CHUNKS), pv,
                                        mix_hi[:, c.slot, 0:4, :].bitcast(F32).rearrange(view, c=CHUNKS),
                                        ALU.subtract).then_inc(attn_lo_ok, 1)

            def rotate(n):
                tok = n.tokens()
                after(dve, qr_ok, n.t)
                dve.wait_ge(rk_ps, n.t + 1)
                nc.vector.tensor_tensor(qk_sin[:, 4, :], rk, sin[:, tok], ALU.mult).then_inc(sin_qk_ok, 1)
                dve.wait_ge(rq_ps, n.t + 1)
                nc.vector.tensor_tensor(qk_sin[:, 0:4, :], rq[:, :, :], each(sin[:, tok], 4), ALU.mult).then_inc(sin_qk_ok, 1)

            def centre(n):
                dve.wait_ge(mean_ps, n.t + 1)
                after(dve, cact_seq, 4 * n.t - 2)
                nc.vector.tensor_tensor(cc[:, :, :], conv_in[:, n.slot, :, :], each(mean, CT), ALU.subtract).then_inc(centre_ok, 1)

            def row_stats(p):
                seq = Count(ln_seq, dve)
                seq.base = p.t * 6
                dve.wait_ge(resid_ok, p.t + 1)
                for a in range(2):
                    seq.inc(nc.vector.bn_stats(stat[:, a, :], r[:, p.slot, a * BLK:(a + 1) * BLK]))
                seq.wait()
                dve.sem_inc(stats_seen, 1)
                seq.inc(nc.vector.bn_aggr(mv[:], stat[:].rearrange("p a s -> p (a s)")))
                seq.wait()
                nc.vector.tensor_scalar(lv[:], mv[:, 1:2], EPS, None, ALU.add).then_inc(lv_ok, 1)

            def row_norm(p):
                seq = Count(ln_seq, dve)
                seq.base, seq.n = p.t * 6, 3
                dve.wait_ge(ly_ok, p.t + 1)
                refine_rstd(nc, seq, lr[:], lv[:], ly[:], lt[:])
                seq.wait()
                nc.vector.tensor_scalar(r[:, p.slot, :], r[:, p.slot, :], mv[:, 0:1], lr[:], ALU.subtract, ALU.mult).then_inc(norm_ok, 1)
                assert seq.n == 6

            def soft_at(n, g, k):
                return n.t * (NKV * 5) + (3 * g + k)

            def soft_shift(n, g):
                dve.wait_ge(score_ps, NKV * n.t + (g + 1))
                if isinstance(n.t, int) and n.t == 0:
                    nc.vector.memset(score[g][:, 0:2, 0:CHUNK], MASKED).then_inc(pads_ok, 1)
                    dve.wait_ge(pads_ok, 5 + g)
                nc.vector.tensor_reduce(top[:, g, :], score[g][:, :, :], AX.X, ALU.max).then_inc(soft_seq, 1)
                dve.wait_ge(soft_seq, soft_at(n, g, 1))
                nc.vector.scalar_tensor_tensor(out=peak[:, g, :], in0=top[:, g, :], scalar=SCALE, in1=sink[:, g, :], op0=ALU.mult,
                                               op1=ALU.max).then_inc(soft_seq, 1)
                dve.wait_ge(soft_seq, soft_at(n, g, 2))
                after(dve, probT_ps, NKV * n.t)
                nc.vector.tensor_tensor(prob[:, g, :, KEYS], sink[:, g, :], peak[:, g, :], ALU.subtract).then_inc(soft_seq, 1)
                nc.vector.scalar_tensor_tensor(out=prob[:, g, :, 0:KEYS], in0=score[g][:, :, :], scalar=SCALE,
                                               in1=along(peak[:, g, :], KEYS), op0=ALU.mult, op1=ALU.subtract).then_inc(shift_ok, 1)

            def soft_norm(n, g):
                dve.wait_ge(exp_ok, NKV * n.t + (g + 1))
                nc.vector.tensor_reduce(den[:, g, :], prob[:, g, :, :], AX.X, ALU.add).then_inc(soft_seq, 1)
                dve.wait_ge(soft_seq, n.t * (NKV * 5) + (3 * NKV + 2 * g + 1))
                nc.vector.reciprocal(inv[:, g, :], den[:, g, :]).then_inc(soft_seq, 1)
                dve.wait_ge(soft_seq, n.t * (NKV * 5) + (3 * NKV + 2 * g + 2))
                nc.vector.tensor_tensor(prob[:, g, :, 0:KEYS], prob[:, g, :, 0:KEYS], along(inv[:, g, :], KEYS), ALU.mult).then_inc(prob_ok, 1)

            def take_v(n):
                dve.wait_ge(vT_ps, n.t + 1)
                after(dve, pv_ps, n.t)
                nc.vector.tensor_copy(vw[:, :, :], vT).then_inc(vw_ok, 1)

            def conv_norm(n):
                seq = Count(cn_seq, dve)
                seq.base = n.t * 4
                dve.wait_ge(cy_ok, n.t + 1)
                seq.inc(nc.vector.tensor_scalar(cv[:], var, EPS, None, ALU.add))
                refine_rstd(nc, seq, cr[:], cv[:], cy[:], ct[:])
                seq.wait()
                assert seq.n == 4
                nc.vector.tensor_tensor(cc[:, :, :], cc[:, :, :], each(cr[:], CT), ALU.mult).then_inc(cn_ok, 1)

            def log_gate(n):
                dve.wait_ge(gate_ok, n.t + 1)
                nc.vector.scalar_tensor_tensor(out=ce[:, :, :], in0=cz[:, :, :], scalar=0.0, in1=ce[:, :, :],
                                               op0=ALU.min, op1=ALU.subtract).then_inc(z_seq, 1)

            def swish(n):
                dve.wait_ge(gate_exp_ok, n.t + 1)
                after(dve, conv_lo_ok, n.t)
                nc.vector.tensor_tensor(sw[:, :, :], cz[:, :, :], ce[:, :, :], ALU.mult).then_inc(swish_ok, 1)

            def conv_lo(n):
                dve.wait_ge(conv_hi_ok, n.t + 1)
                nc.vector.tensor_tensor(mix_lo[:, n.slot, 4:8, :], sw[:, :, :], mix_hi[:, n.slot, 4:8, :].bitcast(F32),
                                        ALU.subtract).then_inc(conv_lo_ok, 1)

            def step(p, c, n):
                rotate(n)
                centre(n)
                if c is None:
                    wo_lo_of(range(WO_POOL[0]))
                if p is not None:
                    row_stats(p)
                if c is not None:
                    log_gate(c)
                soft_shift(n, 0)
                if c is not None:
                    swish(c)
                soft_shift(n, 1)
                if c is not None:
                    conv_lo(c)
                if p is not None:
                    row_norm(p)
                take_v(n)
                soft_norm(n, 0)
                soft_norm(n, 1)
                conv_norm(n)
                if c is not None:
                    residual(c)
                attn_lo(n)

            def last(p, c):
                log_gate(c)
                swish(c)
                conv_lo(c)
                row_stats(p)
                row_norm(p)
                residual(c)

            def final(p):
                row_stats(p)
                row_norm(p)

            def first(n):
                step(None, None, n)
                wo_lo_of(range(WO_POOL[-1] + 1, KT))

            steps(dve, first, step, last, final)

        @block.tensor
        def _(pe):
            pe.wait_ge(con_ld, 16 * 6)
            pe.wait_ge(pads_ok, 4)

            def rotate_and_mean(n):
                pe.wait_ge(in_ld[n.slot], n.nth * 80 + 80)
                after(pe, cn_ok, n.t)
                after(pe, sin_qk_ok, 2 * n.t)
                nc.tensor.matmul(rk, rot[:], qk_in[:, n.slot, 4, :], start=True, stop=True).then_inc(rk_ps, 1)
                nc.tensor.matmul(rq[:, :, :], rot[:], qk_in[:, n.slot, 0:4, :], start=True, stop=True).then_inc(rq_ps, 1)
                pe.wait_ge(sin_qk_ok, 2 * n.t + 1)
                for j in range(CT):
                    m = nc.tensor.matmul(mean, ones[:], conv_in[:, n.slot, j, :], start=j == 0, stop=j == CT - 1)
                m.then_inc(mean_ps, 1)

            def scores(n):
                pe.wait_ge(kr_ok, n.t + 1)
                pe.wait_ge(qr_ok, n.t + 1)
                after(pe, attn_lo_ok, n.t)
                after(pe, shift_ok, NKV * n.t)
                for g in range(NKV):
                    at = slice(HEAD * g, HEAD * (g + 1))
                    for c in range(CHUNKS):
                        for a in range(2):
                            m = nc.tensor.matmul(score[g][:, 2 * c + a, :], qr[at, c, 2 * CHUNK * a:2 * CHUNK * (a + 1)],
                                                 kr[at, CHUNK * c:CHUNK * c + KEYS], start=True, stop=True)
                    m.then_inc(score_ps, 1)

            def variance_and_values(n):
                pe.wait_ge(centre_ok, n.t + 1)
                pe.wait_ge(square_ok, n.t + 1)
                for j in range(CT):
                    m = nc.tensor.matmul(var, ones[:], squares[:, j, :], start=j == 0, stop=j == CT - 1)
                m.then_inc(var_ps, 1)
                after(pe, probT_ok, NKV * n.t)
                after(pe, h1T_ok, n.t - 1)
                for c in range(CHUNKS):
                    m = nc.tensor.transpose(vT[:, c, :], v_in[:, n.slot, CHUNK * c:CHUNK * c + KEYS], ident[:])
                m.then_inc(vT_ps, 1)

            def project(c, ks):
                for k in ks:
                    if k == 0:
                        pe.wait_ge(attn_lo_ok, c.t + 1)
                        after(pe, resid_ok, c.t)
                    if k == 4:
                        pe.wait_ge(conv_lo_ok, c.t + 1)
                    if isinstance(c.t, int) and c.t == 0:
                        if k in WO_POOL:
                            pe.wait_ge(wo_lo_pool_ok, k - WO_POOL[0] + 1)
                        else:
                            pe.wait_ge(wo_lo_ok, k + 1 if k < WO_POOL[0] else k + 1 - len(WO_POOL))
                    for a, w in ((mix_hi, wo_hi), (mix_hi, wo_lo), (mix_lo, wo_hi)):
                        for half in range(2):
                            at = slice(half * BLK, (half + 1) * BLK)
                            m = nc.tensor.matmul(y[:, at], a[:, c.slot, k, :], w[:, k, at],
                                                 start=(k == 0 and w is wo_hi and a is mix_hi),
                                                 stop=(k == KT - 1 and a is mix_lo))
                if ks[-1] == KT - 1:
                    m.then_inc(y_ps, 1)

            def h1_transposes(p, probs_out):
                pe.wait_ge(h1_ok, p.t + 1)
                pe.wait_ge(probT_ok, probs_out)
                for k in range(KT):
                    m = nc.tensor.transpose(tps[:, k * P:(k + 1) * P], r[:, p.slot, k * P:(k + 1) * P], ident[:])
                m.then_inc(h1T_ps, 1)

            def prob_transposes(n, b):
                pe.wait_ge(prob_ok, NKV * n.t + (b + 1))
                for g in range(GROUPS):
                    m = nc.tensor.transpose(tps[:, b * BLK + g * P:b * BLK + (g + 1) * P], prob[:, b, g, 0:KEYS], ident[:])
                m.then_inc(probT_ps, 1)

            def values(n):
                for g in range(NKV):
                    pe.wait_ge(probT_ok, NKV * n.t + (g + 1))
                    for c in range(CHUNKS):
                        m = nc.tensor.matmul(pv[HEAD * g:HEAD * (g + 1), c, :, :], vw[:, c, HEAD * g:HEAD * (g + 1)],
                                             probT[:, g, 2 * P * c:2 * P * (c + 1)], start=True, stop=True)
                m.then_inc(pv_ps, 1)

            def step(p, c, n):
                rotate_and_mean(n)
                if c is not None:
                    project(c, (0, 1))
                scores(n)
                variance_and_values(n)
                if c is not None:
                    project(c, (2, 3, 4, 5, 6))
                pe.wait_ge(vw_ok, n.t + 1)
                prob_transposes(n, 0)
                prob_transposes(n, 1)
                if c is not None:
                    project(c, (7,))
                values(n)
                if p is not None:
                    h1_transposes(p, NKV * (p.t + 3))

            def last(p, c):
                project(c, range(KT))
                h1_transposes(p, NKV * NT)

            def final(p):
                pe.wait_ge(h1_ok, p.t + 1)
                pe.wait_ge(h1T_ok, p.t + 1)
                for k in range(KT):
                    m = nc.tensor.transpose(tps[:, k * P:(k + 1) * P], r[:, p.slot, k * P:(k + 1) * P], ident[:])
                m.then_inc(h1T_ps, 1)

            steps(pe, lambda n: step(None, None, n), step, last, final)


def phase_up(nc, par, w_tiles, h1T_scr, act_scr):
    ctx = ExitStack()
    with ctx:
        def sb(name, shape, dt=F32):
            return ctx.enter_context(nc.sbuf_tensor(name, shape, dt))

        def sem(name):
            return ctx.enter_context(nc.semaphore(name))

        hT_hi = sb("u_hT_hi", [P, KT, SEQ], F32R)
        hT_lo = sb("u_hT_lo", [P, KT, SEQ], F32R)
        w_raw = sb("u_w_raw", [P, 2, KT, P])
        w_hi = sb("u_w_hi", [P, 2, KT, P], F32R)
        w_lo = sb("u_w_lo", [P, 2, KT, P], F32R)
        PAD = FTAPS - 1
        z = sb("u_z", [P, 2, PAD + SEQ])
        y = sb("u_y", [P, 2, SEQ])
        stage = y[:, :, :].rearrange("p s (k t) -> p s k t", k=KT // 2)
        taps = sb("u_taps", [P, 2 * FT, FTAPS])
        bias = sb("u_bias", [P, 2 * FT])
        mm = [[ctx.enter_context(nc.psum_tensor(f"u_mm{m}{n}", [P, BLK], F32)) for n in range(NB)] for m in range(2)]

        par_ld = sem("u_par_ld")
        w_ld = [sem(f"u_w_ld{s}") for s in range(2)]
        h_ld = [sem(f"u_h_ld{s}") for s in range(2)]
        hi_ok, lo_ok, whi_ok, wlo_ok = sem("u_hi"), sem("u_lo"), sem("u_whi"), sem("u_wlo")
        mm_ok, z_ok, pad_ok, conv_seq, conv_ok = sem("u_mm"), sem("u_z_ok"), sem("u_pad"), sem("u_conv_seq"), sem("u_conv")
        gelu_ok, act_ok, act_st = sem("u_gelu"), sem("u_act"), sem("u_act_st")
        last_ok = sem("u_last")
        block = ctx.enter_context(nc.Block())

        def products_count(j, m, n):
            return 2 * NB * j + (NB * m + n)

        @block.sync
        def _(sp):
            for q in range(2 * NB):
                if q < 2:
                    sp.dma_start(w_raw[:, q, :, :], w_tiles[q, :, :, :]).then_inc(w_ld[q], 16)
                else:
                    sp.wait_ge(lo_ok, q - 1)
                src = h1T_scr[(q % 2) * KT // 2:(q % 2 + 1) * KT // 2, :, bass.ts(q // 2, BLK)]
                sp.dma_start(stage[:, q % 2, :, :], src.rearrange("k p t -> p k t")).then_inc(h_ld[q % 2], 16)
                if q == 1:
                    sp.dma_start(taps[:, :, :], par[:, PAR_FTAPS:PAR_FB].rearrange("p (c t) -> p c t", t=FTAPS)).then_inc(par_ld, 16)
                    sp.dma_start(bias[:], par[:, PAR_FB:PAR_SINK]).then_inc(par_ld, 16)

            def store(j):
                sp.wait_ge(act_ok, j + 1)
                sp.dma_start(act_scr[bass.ds(j, 1), :, :].rearrange("o p t -> p (o t)"), y[:, 1, :]).then_inc(act_st, 16)

            with sp.Fori(1, FT) as j:
                for m in range(2):
                    sp.wait_ge(wlo_ok, 2 * j + (m - 1))
                    sp.dma_start(w_raw[:, m, :, :], w_tiles[bass.ds(2 * j + m, 1), :, :, :].rearrange("o p k c -> p (o k) c")).then_inc(w_ld[m], 16)
                store(j - 1)
            for n in range(NB):
                sp.wait_ge(last_ok, n + 1)
                sp.dma_start(act_scr[FT - 1, :, bass.ts(n, BLK)], y[:, 1, bass.ts(n, BLK)]).then_inc(act_st, 16)
            sp.wait_ge(act_st, 16 * (FT - 1 + NB))

        @block.gpsimd
        def _(pool):
            nc.gpsimd.memset(z[:, :, 0:PAD], 0.0).then_inc(pad_ok, 1)

        @block.scalar
        def _(act):
            def weights_hi(nth, slot):
                act.wait_ge(w_ld[slot], nth * 16)
                nc.scalar.copy(w_hi[:, slot, :, :], w_raw[:, slot, :, :]).then_inc(whi_ok, 1)

            def take(count, m, n):
                act.wait_ge(mm_ok, count + 1)
                nc.scalar.copy(z[:, m, bass.ds(PAD + n * BLK, BLK)], mm[m][n][:]).then_inc(z_ok, 1)

            def gelu(j):
                act.wait_ge(conv_ok, 2 * j + 1)
                nc.scalar.activation(y[:, 0, :], y[:, 0, :], ACT.Gelu).then_inc(gelu_ok, 1)

            nc.scalar.preload_act_table(ACT.Gelu)
            for q in range(2 * NB):
                if q < 2:
                    weights_hi(1, q)
                act.wait_ge(h_ld[q % 2], 16 * (q // 2 + 1))
                at = slice((q % 2) * KT // 2, (q % 2 + 1) * KT // 2)
                nc.scalar.copy(hT_hi[:, at, bass.ts(q // 2, BLK)], stage[:, q % 2, :, :]).then_inc(hi_ok, 1)
                if q % 2 and q > 1:
                    for m in range(2):
                        take(q - 3 + m, m, q // 2 - 1)
            for m in range(2):
                take(2 * NB - 2 + m, m, NB - 1)
                weights_hi(2, m)
            gelu(0)

            def pair(j, last):
                act.wait_ge(conv_ok, 2 * j - 1)
                for n in range(NB):
                    take(products_count(j, 0, n), 0, n)
                if not last:
                    weights_hi(j + 2, 0)
                act.wait_ge(conv_ok, 2 * j)
                for n in range(NB):
                    take(products_count(j, 1, n), 1, n)
                    if n == 1:
                        gelu(j)
                if not last:
                    weights_hi(j + 2, 1)

            with act.Fori(1, FT - 1) as j:
                pair(j, False)
            pair(FT - 1, True)

        @block.vector
        def _(dve):
            def weights_lo(s, slot):
                dve.wait_ge(whi_ok, s + 1)
                nc.vector.tensor_tensor(w_lo[:, slot, :, :], w_raw[:, slot, :, :], w_hi[:, slot, :, :].bitcast(F32),
                                        ALU.subtract).then_inc(wlo_ok, 1)

            def tap(s, k):
                return taps[:, bass.ds(s, 1), k:k + 1].rearrange("p o t -> p (o t)")

            def convolve(j, m):
                s, steps = 2 * j + m, FTAPS - 1
                dve.wait_ge(z_ok, NB * s + NB)
                nc.vector.tensor_scalar(y[:, m, :], z[:, m, PAD:], tap(s, PAD), bias[:, bass.ds(s, 1)], ALU.mult,
                                        ALU.add).then_inc(conv_seq, 1)
                for k in range(PAD):
                    dve.wait_ge(conv_seq, steps * s + (k + 1))
                    v = nc.vector.scalar_tensor_tensor(out=y[:, m, :], in0=z[:, m, k:k + SEQ], scalar=tap(s, k),
                                                       in1=y[:, m, :], op0=ALU.mult, op1=ALU.add)
                    v.then_inc(conv_seq if k < PAD - 1 else conv_ok, 1)

            def last_value():
                s, base = 2 * FT - 1, (FTAPS - 1) * (2 * FT - 1)
                for n in range(NB):
                    at = slice(n * BLK, (n + 1) * BLK)
                    dve.wait_ge(z_ok, NB * s + n + 1)
                    nc.vector.tensor_scalar(y[:, 1, at], z[:, 1, PAD + n * BLK:PAD + (n + 1) * BLK], tap(s, PAD),
                                            bias[:, s:s + 1], ALU.mult, ALU.add).then_inc(conv_seq, 1)
                    for k in range(PAD):
                        dve.wait_ge(conv_seq, base + (PAD + 1) * n + (k + 1))
                        nc.vector.scalar_tensor_tensor(out=y[:, 1, at], in0=z[:, 1, n * BLK + k:(n + 1) * BLK + k], scalar=tap(s, k),
                                                       in1=y[:, 1, at], op0=ALU.mult, op1=ALU.add).then_inc(conv_seq, 1)
                    dve.wait_ge(conv_seq, base + (PAD + 1) * (n + 1))
                    dve.wait_ge(gelu_ok, FT)
                    nc.vector.tensor_tensor(y[:, 1, at], y[:, 1, at], y[:, 0, at], ALU.mult).then_inc(last_ok, 1)

            def gated(j):
                dve.wait_ge(gelu_ok, j + 1)
                dve.wait_ge(conv_ok, 2 * j + 2)
                nc.vector.tensor_tensor(y[:, 1, :], y[:, 1, :], y[:, 0, :], ALU.mult).then_inc(act_ok, 1)

            for q in range(2 * NB):
                if q < 2:
                    weights_lo(q, q)
                dve.wait_ge(hi_ok, q + 1)
                at = slice((q % 2) * KT // 2, (q % 2 + 1) * KT // 2)
                nc.vector.tensor_tensor(hT_lo[:, at, bass.ts(q // 2, BLK)], stage[:, q % 2, :, :],
                                        hT_hi[:, at, bass.ts(q // 2, BLK)].bitcast(F32), ALU.subtract).then_inc(lo_ok, 1)
            dve.wait_ge(par_ld, 32)
            dve.wait_ge(pad_ok, 1)
            weights_lo(2, 0)
            weights_lo(3, 1)
            convolve(0, 0)
            convolve(0, 1)
            gated(0)

            def pair(j, last):
                dve.wait_ge(act_ok, j)
                convolve(j, 0)
                if not last:
                    weights_lo(2 * j + 2, 0)
                dve.wait_ge(act_st, 16 * j)
                if last:
                    last_value()
                    return
                convolve(j, 1)
                gated(j)
                weights_lo(2 * j + 3, 1)

            with dve.Fori(1, FT - 1) as j:
                pair(j, False)
            pair(FT - 1, True)

        @block.tensor
        def _(pe):
            def products(m, n, ks=range(KT)):
                for k in ks:
                    for w, h in ((w_hi, hT_hi), (w_hi, hT_lo), (w_lo, hT_hi)):
                        last = nc.tensor.matmul(mm[m][n][:], w[:, m, k, :], h[:, k, bass.ts(n, BLK)],
                                                start=(k == 0 and w is w_hi and h is hT_hi),
                                                stop=(k == KT - 1 and w is w_lo))
                if ks[-1] == KT - 1:
                    last.then_inc(mm_ok, 1)

            for q in range(2):
                pe.wait_ge(lo_ok, q + 1)
                for m in range(2):
                    pe.wait_ge(wlo_ok, m + 1)
                    products(m, 0, range(q * KT // 2, (q + 1) * KT // 2))
            for n in range(1, NB):
                pe.wait_ge(lo_ok, 2 * n + 2)
                for m in range(2):
                    products(m, n)
            with pe.Fori(1, FT) as j:
                for m in range(2):
                    pe.wait_ge(wlo_ok, 2 * j + (m + 1))
                    for n in range(NB):
                        pe.wait_ge(z_ok, products_count(j, m, n) - 3)
                        products(m, n)


def phase_down(nc, w_down, ln_g, ln_b, act_scr, h1_scr, out):
    ctx = ExitStack()
    with ctx:
        def sb(name, shape, dt=F32):
            return ctx.enter_context(nc.sbuf_tensor(name, shape, dt))

        def sem(name):
            return ctx.enter_context(nc.semaphore(name))

        RAW = 3
        wd_hi = sb("d_wd_hi", [P, HALF, D], F32R)
        wd_lo = sb("d_wd_lo", [P, HALF, D], F32R)
        wd_raw = sb("d_wd_raw", [P, RAW, D])
        total = sb("d_total", [P, NT, D])
        a_raw = sb("d_a_raw", [P, 2, HALF, P])
        a_hi = sb("d_a_hi", [P, 2, HALF, P], F32R)
        a_lo = sb("d_a_lo", [P, 2, HALF, P], F32R)
        g_bc, b_bc = sb("d_g", [P, D]), sb("d_b", [P, D])
        stat, mv = sb("d_stat", [P, 2, 6]), sb("d_mv", [P, 2])
        lv, ls, ly, lt, lr = (sb(f"d_l{k}", [P, 1]) for k in range(5))
        y = [ctx.enter_context(nc.psum_tensor(f"d_y{s}", [P, D], F32)) for s in range(2)]

        wd_ld = [sem(f"d_wd_ld{s}") for s in range(RAW)]
        a_ld = [sem(f"d_a_ld{s}") for s in range(2)]
        row_ld, out_st = sem("d_row_ld"), sem("d_out_st")
        h1_ld = [sem(f"d_h1_ld{s}") for s in range(2)]
        whi_ok, wlo_ok, used_ok = sem("d_whi"), sem("d_wlo"), sem("d_used")
        ahi_ok, alo_ok, y_ok, sum_ok = sem("d_ahi"), sem("d_alo"), sem("d_y_ok"), sem("d_sum")
        ln_seq, lv_ok, ls_ok, norm_ok, scaled_ok, out_ok = (sem("d_" + n) for n in ("ln_seq", "lv", "ls", "norm", "scaled", "out"))
        stats_seen, pool_seen = sem("d_stats_seen"), sem("d_pool_seen")
        block = ctx.enter_context(nc.Block())

        def run(eng, step):
            for f in range(2):
                step(NT * f, 0, f, 0, NT // 2 * f + 1, "first")
                with eng.Fori(0, NT // 2 - 1) as i:
                    step(2 * i + (NT * f + 1), 2 * i + 1, f, 1, i + (NT // 2 * f + 2), "")
                    step(2 * i + (NT * f + 2), 2 * i + 2, f, 0, i + (NT // 2 * f + 2), "")
                step(NT * f + NT - 1, NT - 1, f, 1, NT // 2 * f + NT // 2 + 1, "last")

        def tile_of(t):
            return total[:, bass.ds(t, 1), :].rearrange("p o d -> p (o d)")

        def tokens(t):
            return bass.ds(t * P, P)

        @block.sync
        def _(sp):
            def load_act(t, f, slot):
                sp.dma_start(a_raw[:, slot, :, :], act_scr[HALF * f:HALF * (f + 1), :, tokens(t)].rearrange("k p t -> p k t")).then_inc(a_ld[slot], 16)

            def load_wd(k):
                if k >= RAW:
                    sp.wait_ge(wlo_ok, k - RAW + 1)
                sp.dma_start(wd_raw[:, k % RAW, :], w_down[k, :, :]).then_inc(wd_ld[k % RAW], 16)

            load_act(0, 0, 0)
            for k in range(HALF):
                load_wd(k)
                if k == HALF // 2:
                    load_act(1, 0, 1)
            sp.dma_start(g_bc[:], row_to_all(ln_g)).then_inc(row_ld, 16)
            sp.dma_start(b_bc[:], row_to_all(ln_b)).then_inc(row_ld, 16)

            def load_h1(t, slot):
                sp.dma_start(tile_of(t), h1_scr[bass.ds(t, 1), :, :].rearrange("o p d -> p (o d)")).then_inc(h1_ld[slot], 16)

            def step(u, t, f, slot, nth, at):
                if f == 0 and at != "first":
                    sp.wait_ge(alo_ok, u)
                    load_h1(t - 1, 1 - slot)
                if f == 0 and at == "last":
                    load_act(0, 1, 1 - slot)
                    for k in range(HALF, 2 * HALF):
                        load_wd(k)
                    sp.wait_ge(alo_ok, NT)
                    load_h1(t, slot)
                elif at != "last" and (f or at != "first"):
                    sp.wait_ge(alo_ok, u)
                    load_act(t + 1, f, 1 - slot)

            run(sp, step)

        @block.gpsimd
        def _(pool):
            pool.wait_ge(row_ld, 32)
            with pool.Fori(0, NT) as t:
                pool.wait_ge(norm_ok, t + 1)
                pool.sem_inc(pool_seen, 1)
                nc.gpsimd.tensor_tensor(tile_of(t), tile_of(t), g_bc[:], ALU.mult).then_inc(scaled_ok, 1)
                pool.wait_ge(scaled_ok, t + 1)
                pool.sem_inc(pool_seen, 1)
                nc.gpsimd.tensor_tensor(tile_of(t), tile_of(t), b_bc[:], ALU.add).then_inc(out_ok, 1)

        @block.scalar
        def _(act):
            def act_hi(u, slot, nth):
                act.wait_ge(a_ld[slot], nth * 16)
                after(act, y_ok, u - 1)
                nc.scalar.copy(a_hi[:, slot, :, :], a_raw[:, slot, :, :]).then_inc(ahi_ok, 1)

            def wd_hi_of(k):
                act.wait_ge(wd_ld[k % RAW], 16 * (k // RAW + 1))
                if k >= HALF:
                    if k < 2 * HALF - 1:
                        act.wait_ge(used_ok, k - HALF + 1)
                    else:
                        act.wait_ge(y_ok, NT)
                nc.scalar.copy(wd_hi[:, k % HALF, :], wd_raw[:, k % RAW, :]).then_inc(whi_ok, 1)

            def root(t):
                act.wait_ge(lv_ok, t + 1)
                nc.scalar.activation(ls[:], lv[:], ACT.Sqrt).then_inc(ls_ok, 1)

            def store(t):
                act.wait_ge(out_ok, t + 1)
                act.dma_start(out[0, tokens(t), :], tile_of(t)).then_inc(out_st, 16)

            nc.scalar.preload_act_table(ACT.Sqrt)
            act_hi(0, 0, 1)
            for k in range(HALF):
                wd_hi_of(k)

            def step(u, t, f, slot, nth, at):
                if not (f == 1 and at == "last"):
                    act_hi(u + 1, 1 - slot, nth)
                if f == 0 and at == "last":
                    for k in range(HALF, 2 * HALF):
                        wd_hi_of(k)
                if f == 1 and at != "first":
                    root(t - 1)
                    store(t - 1)

            run(act, step)
            root(NT - 1)
            store(NT - 1)
            act.wait_ge(out_st, 16 * NT)

        @block.vector
        def _(dve):
            def act_lo(u, slot):
                dve.wait_ge(ahi_ok, u + 1)
                nc.vector.tensor_tensor(a_lo[:, slot, :, :], a_raw[:, slot, :, :], a_hi[:, slot, :, :].bitcast(F32),
                                        ALU.subtract).then_inc(alo_ok, 1)

            def wd_lo_of(k):
                dve.wait_ge(whi_ok, k + 1)
                nc.vector.tensor_tensor(wd_lo[:, k % HALF, :], wd_raw[:, k % RAW, :], wd_hi[:, k % HALF, :].bitcast(F32),
                                        ALU.subtract).then_inc(wlo_ok, 1)

            def add(u, t, f, slot, uses):
                dve.wait_ge(y_ok, u + 1)
                if f == 0:
                    dve.wait_ge(h1_ld[slot], 16 * uses)
                nc.vector.scalar_tensor_tensor(out=tile_of(t), in0=tile_of(t), scalar=ALPHA if f == 0 else 1.0, in1=y[slot][:],
                                               op0=ALU.mult, op1=ALU.add).then_inc(sum_ok, 1)

            def norm(t):
                seq = Count(ln_seq, dve)
                seq.base = t * 7
                dve.wait_ge(sum_ok, t + (NT + 2))
                dve.sem_inc(stats_seen, 1)
                for a in range(2):
                    seq.inc(nc.vector.bn_stats(stat[:, a, :], tile_of(t)[:, a * BLK:(a + 1) * BLK]))
                seq.wait()
                dve.sem_inc(stats_seen, 1)
                seq.inc(nc.vector.bn_aggr(mv[:], stat[:].rearrange("p a s -> p (a s)")))
                seq.wait()
                nc.vector.tensor_scalar(lv[:], mv[:, 1:2], EPS, None, ALU.add).then_inc(lv_ok, 1)
                dve.wait_ge(ls_ok, t + 1)
                seq.inc(nc.vector.reciprocal(ly[:], ls[:]))
                refine_rstd(nc, seq, lr[:], lv[:], ly[:], lt[:])
                seq.wait()
                assert seq.n == 7
                nc.vector.tensor_scalar(tile_of(t), tile_of(t), mv[:, 0:1], lr[:], ALU.subtract, ALU.mult).then_inc(norm_ok, 1)

            dve.sem_inc(sum_ok, 1)
            act_lo(0, 0)
            for k in range(HALF):
                wd_lo_of(k)

            def step(u, t, f, slot, nth, at):
                if at == "first" and f == 1:
                    add(NT - 1, NT - 1, 0, 1 - slot, NT // 2)
                elif at != "first":
                    uses = nth - NT // 2 * f - 1
                    add(u - 1, t - 1, f, 1 - slot, uses)
                if not (f == 1 and at == "last"):
                    act_lo(u + 1, 1 - slot)
                if f == 0 and at == "last":
                    for k in range(HALF, 2 * HALF):
                        wd_lo_of(k)
                if f == 1 and at != "first":
                    norm(t - 1)

            run(dve, step)
            add(2 * NT - 1, NT - 1, 1, 1, NT // 2)
            norm(NT - 1)

        @block.tensor
        def _(pe):
            def step(u, t, f, slot, nth, at):
                pe.wait_ge(alo_ok, u + 1)
                after(pe, sum_ok, u)
                for k in range(HALF):
                    if at == "first":
                        pe.wait_ge(wlo_ok, HALF * f + k + 1)
                    for a, w in ((a_hi, wd_hi), (a_hi, wd_lo), (a_lo, wd_hi)):
                        for half in range(2):
                            cols = slice(half * BLK, (half + 1) * BLK)
                            m = nc.tensor.matmul(y[slot][:, cols], a[:, slot, k, :], w[:, k, cols],
                                                 start=(k == 0 and a is a_hi and w is wd_hi),
                                                 stop=(k == HALF - 1 and a is a_lo))
                    if f == 0 and at == "last" and k < HALF - 1:
                        m.then_inc(used_ok, 1)
                m.then_inc(y_ok, 1)

            run(pe, step)


def build(nc, io, out):
    def scratch(name, shape):
        return nc.dram_tensor(name, shape, F32, kind="Internal").ap()

    h, h1 = scratch("h_scr", (NT, P, D)), scratch("h1_scr", (NT, P, D))
    qkv, conv = scratch("qkv_scr", (QT, P, SEQ)), scratch("conv_scr", (CT, P, SEQ))
    h1T, gated = scratch("h1T_scr", (KT, P, SEQ)), scratch("gated_scr", (FT, P, SEQ))
    trig = scratch("trig_scr", (2, ROT // 2, SEQ))
    phase_project(nc, io["x"], io["positions"], io["in_ln_g"], io["in_ln_b"], io["w_in"], io["par"], io["con"], h, qkv, conv, trig)
    phase_mix(nc, trig, io["par"], io["con"], io["w_o"], io["ln1_g"], io["ln1_b"], h, qkv, conv, h1, h1T)
    phase_up(nc, io["par"], io["w_up"], h1T, gated)
    phase_down(nc, io["w_down"], io["ln2_g"], io["ln2_b"], gated, h1, out)


def lay_out(v):
    a = {k: np.asarray(w) for k, w in v.items()}

    def columns(w, tiles):
        t = w.reshape(KT, P, w.shape[1] // P, P).transpose(2, 1, 0, 3)
        return np.ascontiguousarray(t[tiles])

    def channels(w):
        return w.reshape(w.shape[0], -1, P).transpose(2, 1, 0).reshape(P, -1)

    ffn_order = [t for j in range(FT) for t in (j, FT + j)]
    ftaps = a["ffn_conv_w"][0].reshape(FTAPS, 2 * FT, P).transpose(2, 1, 0)[:, ffn_order].reshape(P, -1)
    fbias = a["ffn_conv_b"][0].reshape(2 * FT, P).T[:, ffn_order]
    pairs = np.repeat(a["sinks"][0].reshape(NKV, 2, 2), CHUNK, axis=2)
    sinks = np.tile(pairs[:, None], (1, CHUNKS, 1, 1)).reshape(NKV * GROUPS, P).T
    par = np.concatenate([channels(a["conv_w"][0]), channels(a["conv_b"]), channels(a["conv_ln_g"]),
                          channels(a["conv_ln_b"]), ftaps, fbias, sinks], axis=1)
    assert par.shape == (P, PAR_N)
    w_o = a["w_o"][0]
    heads = w_o[:DC].reshape(2, NQ // 2, HEAD, D).transpose(1, 0, 2, 3).reshape(NQ // 2, P, D)
    con = np.zeros((P, CON_N), np.float32)
    con[:, CON_ID:CON_ID + P] = np.eye(P)
    for base in (0, HEAD):
        for i in range(ROT // 2):
            con[base + ROT // 2 + i, CON_ROT + base + i] = -1.0
            con[base + i, CON_ROT + base + ROT // 2 + i] = 1.0
    con[:, CON_FREQ] = np.repeat(ROPE_THETA ** (-np.arange(ROT // 2) / (ROT // 2)), NT)
    con[:, CON_ONES:CON_ONES + P] = 1 / DC
    return {
        "x": a["x"][0], "positions": a["positions"], "in_ln_g": a["in_ln_g"], "in_ln_b": a["in_ln_b"],
        "w_in": columns(a["w_in"][0], IN_TILES), "w_o": np.ascontiguousarray(
            np.concatenate([heads, w_o[DC:].reshape(CT, P, D)]).transpose(1, 0, 2)),
        "w_up": columns(a["w_up"][0], ffn_order), "w_down": a["w_down"][0].reshape(FT, P, D),
        "ln1_g": a["ln1_g"][0], "ln1_b": a["ln1_b"][0], "ln2_g": a["ln2_g"][0], "ln2_b": a["ln2_b"][0],
        "par": np.ascontiguousarray(par), "con": con,
    }


def kernel(**inputs):
    import concourse.bacc as bacc
    from concourse.bass_utils import run_bass_kernel_spmd

    arrays = lay_out(inputs)
    nc = bacc.Bacc("TRN2", target_bir_lowering=False, num_devices=1)
    io = {k: nc.dram_tensor(k, v.shape, mybir.dt.from_np(v.dtype), kind="ExternalInput").ap() for k, v in arrays.items()}
    out = nc.dram_tensor("out", (1, SEQ, D), F32, kind="ExternalOutput").ap()
    build(nc, io, out)
    r = run_bass_kernel_spmd(nc, [arrays], core_ids=[0])
    return r.results[0]["out"]
```
